# Optimizing a Trainium2 kernel written in Bass

```python
import math
import jax, jax.numpy as jnp
from jax import lax
import numpy as np

D_MODEL = 1024
BATCH = 1
SEQ = 512
DEPTH = 4
DEC_BATCH = 8
DEC_SEQ = 8
PAST_LEN = 256
PAGE_SIZE = 128

N_MIXERS = 3
HEAD_DIM = 64
N_HEADS = D_MODEL // HEAD_DIM
CONV_W = 3
D_FF = ((8 * D_MODEL // 3 + 255) // 256) * 256
Q_BLOCK = 128
DECAY_LORA = max(32, int(round(1.8 * math.sqrt(D_MODEL) / 32)) * 32)
AAA_LORA = max(32, int(round(1.8 * math.sqrt(D_MODEL) / 32)) * 32)
GATE_LORA = max(32, int(round(0.6 * D_MODEL ** 0.8 / 32)) * 32)
RMS_EPS = 1e-6
GN_EPS = 64e-5
SB_BIAS_INIT = -6.0
N_A = (DEPTH + 2) // 3
N_B = (DEPTH + 1) // 3
N_C = DEPTH // 3

kernel_name = 'hybrid_shortconv_stickbreak_rwkv7_step'

def rmsnorm(x, g):
    xf = x.astype(jnp.float32)
    y = xf * lax.rsqrt(jnp.mean(xf * xf, axis=-1, keepdims=True) + RMS_EPS)
    return (y * g.astype(jnp.float32)).astype(x.dtype)

def causal_dwconv(p, buf, w):
    T = p.shape[1]
    pad = jnp.concatenate([buf.astype(p.dtype), p], axis=1)
    out = sum(w[i] * pad[:, i:i + T] for i in range(CONV_W))
    return out, pad[:, T:]

def short_conv_mixer(u, buf, w_in, conv_w, w_out):
    bch = u @ w_in
    b_gate, c_gate, h = jnp.split(bch, 3, axis=-1)
    pc, new_buf = causal_dwconv(c_gate * h, buf, conv_w)
    return (b_gate * pc) @ w_out, new_buf

def conv_ffn(u, buf, w_gu, conv_w, w_down):
    gate, up = jnp.split(u @ w_gu, 2, axis=-1)
    gate_c, new_buf = causal_dwconv(gate, buf, conv_w)
    return (jax.nn.silu(gate_c) * up) @ w_down, new_buf

def _stick_break_block(q_blk, q_pos, keys, vals, k_pos, bias):
    z = jnp.einsum('bqhd,bkhd->bhqk', q_blk, keys).astype(jnp.float32) * (HEAD_DIM ** -0.5)
    z = z + bias.astype(jnp.float32)[None, :, None, None]
    mask = k_pos[None, :] < q_pos[:, None]
    log_stay = jnp.where(mask, jax.nn.log_sigmoid(-z), 0.0)
    between = lax.cumsum(log_stay, axis=3, reverse=True) - log_stay
    a = jnp.where(mask, jnp.exp(jax.nn.log_sigmoid(z) + between), 0.0)
    return jnp.einsum('bhqk,bkhd->bqhd', a.astype(vals.dtype), vals)

def stick_breaking_mixer(u, past_k, past_v, w_qkv, w_o, bias):
    Bn, T, _ = u.shape
    qkv = (u @ w_qkv).reshape(Bn, T, 3, N_HEADS, HEAD_DIM)
    q, k, v = qkv[:, :, 0], qkv[:, :, 1], qkv[:, :, 2]
    if past_k is None:
        keys, vals, P = k, v, 0
    else:
        keys = jnp.concatenate([past_k.astype(k.dtype), k], axis=1)
        vals = jnp.concatenate([past_v.astype(v.dtype), v], axis=1)
        P = past_k.shape[1]
    k_pos = jnp.arange(P + T)
    qb = Q_BLOCK if T % Q_BLOCK == 0 else T
    nb = T // qb
    q_blocks = q.reshape(Bn, nb, qb, N_HEADS, HEAD_DIM).transpose(1, 0, 2, 3, 4)
    q_pos = (P + jnp.arange(T)).reshape(nb, qb)
    o = lax.map(lambda a: _stick_break_block(a[0], a[1], keys, vals, k_pos, bias), (q_blocks, q_pos))
    o = o.transpose(1, 0, 2, 3, 4).reshape(Bn, T, D_MODEL)
    return o @ w_o, k, v

def _wkv_scan(S0, r, w, k, v, a, b):
    def step(S, inp):
        r_t, w_t, k_t, v_t, a_t, b_t = inp
        sa = jnp.einsum('bhij,bhj->bhi', S, a_t)
        S = S * w_t[:, :, None, :] + sa[..., None] * b_t[:, :, None, :] + v_t[..., None] * k_t[:, :, None, :]
        return S, jnp.einsum('bhij,bhj->bhi', S, r_t)
    xs = tuple(jnp.moveaxis(t, 1, 0) for t in (r, w, k, v, a, b))
    S, y = lax.scan(step, S0, xs)
    return jnp.moveaxis(y, 0, 1), S

def rwkv7_mixer(u, shift_buf, S0, mu, w_rkv, w0, w1, w2, a0, a1, a2, g1, g2,
                k_k, k_a, r_k, ln_w, ln_b, w_o):
    Bn, T, D = u.shape
    f32 = jnp.float32
    prev = jnp.concatenate([shift_buf[:, None].astype(u.dtype), u[:, :-1]], axis=1)
    xm = u[None] + (prev - u)[None] * mu[:, None, None, :]
    rkv = jnp.einsum('nbtd,nde->nbte', xm[:3], w_rkv)
    r, k, v = rkv[0], rkv[1], rkv[2]
    wlog = -jax.nn.softplus(-(w0 + jnp.tanh(xm[3] @ w1) @ w2)) - 0.5
    a = jax.nn.sigmoid(a0 + (xm[4] @ a1) @ a2)
    g = jax.nn.sigmoid(xm[5] @ g1) @ g2
    hd = lambda t: t.reshape(Bn, T, N_HEADS, HEAD_DIM).astype(f32)
    decay = jnp.exp(-jnp.exp(hd(wlog)))
    kk = hd(k * k_k)
    kk = kk / jnp.maximum(jnp.sqrt(jnp.sum(kk * kk, axis=-1, keepdims=True)), 1e-12)
    k = k * (1 + (a - 1) * k_a)
    rh, kh, vh, ah = hd(r), hd(k), hd(v), hd(a)
    y, S = _wkv_scan(S0.astype(f32), rh, decay, kh, vh, -kk, kk * ah)
    mean = jnp.mean(y, axis=-1, keepdims=True)
    var = jnp.mean(jnp.square(y - mean), axis=-1, keepdims=True)
    y = ((y - mean) * lax.rsqrt(var + GN_EPS)).reshape(Bn, T, D) * ln_w.astype(f32) + ln_b.astype(f32)
    y = y + (jnp.sum(rh * kh * r_k.astype(f32), axis=-1, keepdims=True) * vh).reshape(Bn, T, D)
    out = (y.astype(u.dtype) * g) @ w_o
    return out, u[:, -1], S.astype(u.dtype)

def trunk(x, c, conv_a_buf, cache_k, cache_v, page_table, wkv0, shift0, ffn_buf, prm):
    Bn = x.shape[0]
    mods = jnp.einsum('bd,lde->lbe', jax.nn.silu(c), prm['ada_w']) + prm['ada_b'][:, None]
    conv_a_new, k_new, v_new, wkv_new, shift_new, ffn_new = [], [], [], [], [], []
    for i in range(DEPTH):
        sh1, sc1, g1, sh2, sc2, g2 = [m[:, None, :] for m in jnp.split(mods[i], 6, axis=-1)]
        u = rmsnorm(x, prm['norm_g'][i, 0]) * (1 + sc1) + sh1
        j = i // N_MIXERS
        kind = i % N_MIXERS
        if kind == 0:
            o, nb = short_conv_mixer(u, conv_a_buf[j], prm['a_w_in'][j], prm['a_conv'][j], prm['a_w_out'][j])
            conv_a_new.append(nb)
        elif kind == 1:
            if cache_k is None:
                pk, pv = None, None
            else:
                pk = cache_k[j][page_table].reshape(Bn, -1, N_HEADS, HEAD_DIM)
                pv = cache_v[j][page_table].reshape(Bn, -1, N_HEADS, HEAD_DIM)
            o, kn, vn = stick_breaking_mixer(u, pk, pv, prm['b_w_qkv'][j], prm['b_w_o'][j], prm['b_bias'][j])
            k_new.append(kn)
            v_new.append(vn)
        else:
            o, sn, Sn = rwkv7_mixer(
                u, shift0[j], wkv0[j], prm['r7_mu'][j], prm['r7_w_rkv'][j], prm['r7_w0'][j],
                prm['r7_w1'][j], prm['r7_w2'][j], prm['r7_a0'][j], prm['r7_a1'][j], prm['r7_a2'][j],
                prm['r7_g1'][j], prm['r7_g2'][j], prm['r7_k_k'][j], prm['r7_k_a'][j], prm['r7_r_k'][j],
                prm['r7_ln_w'][j], prm['r7_ln_b'][j], prm['r7_w_o'][j])
            shift_new.append(sn)
            wkv_new.append(Sn)
        x = x + g1 * rmsnorm(o, prm['norm_g'][i, 1])
        u = rmsnorm(x, prm['norm_g'][i, 2]) * (1 + sc2) + sh2
        o, fb = conv_ffn(u, ffn_buf[i], prm['f_w_gu'][i], prm['f_conv'][i], prm['f_w_down'][i])
        ffn_new.append(fb)
        x = x + g2 * rmsnorm(o, prm['norm_g'][i, 3])
    return (x, jnp.stack(conv_a_new), jnp.stack(k_new), jnp.stack(v_new),
            jnp.stack(wkv_new), jnp.stack(shift_new), jnp.stack(ffn_new))

def setup_inputs(seed: int = 0) -> dict:
    key = jax.random.key(seed)
    keys = iter(jax.random.split(key, 64))
    f32 = jnp.float32

    def nrm(shape, scale=1.0):
        return jax.random.normal(next(keys), shape, f32) * scale

    def unif(shape, lo, hi):
        return jax.random.uniform(next(keys), shape, f32, lo, hi)

    D, H, Dh, F = D_MODEL, N_HEADS, HEAD_DIM, D_FF
    rs = D ** -0.5
    n_pages = PAST_LEN // PAGE_SIZE
    n_used = DEC_BATCH * n_pages
    n_pool = n_used + n_used // 4
    perm = jax.random.permutation(next(keys), n_pool)
    page_table = perm[:n_used].reshape(DEC_BATCH, n_pages).astype(jnp.int32)
    return {
        'x_prompt': nrm((BATCH, SEQ, D)),
        'x_sample': nrm((DEC_BATCH, DEC_SEQ, D)),
        'cache_k': nrm((N_B, n_pool, PAGE_SIZE, H, Dh)),
        'cache_v': nrm((N_B, n_pool, PAGE_SIZE, H, Dh)),
        'page_table': page_table,
        'state_conv_a': nrm((N_A, DEC_BATCH, CONV_W - 1, D)),
        'state_wkv': nrm((N_C, DEC_BATCH, H, Dh, Dh), 0.3),
        'state_shift': nrm((N_C, DEC_BATCH, D)),
        'state_ffn_conv': nrm((DEPTH, DEC_BATCH, CONV_W - 1, F)),
        'c_prompt': nrm((BATCH, D)),
        'c_sample': nrm((DEC_BATCH, D)),
        'ada_w': nrm((DEPTH, D, 6 * D), 0.5 * rs),
        'ada_b': nrm((DEPTH, 6 * D), 0.02),
        'norm_g': 1.0 + nrm((DEPTH, 4, D), 0.02),
        'a_w_in': nrm((N_A, D, 3 * D), rs),
        'a_conv': nrm((N_A, CONV_W, D), CONV_W ** -0.5),
        'a_w_out': nrm((N_A, D, D), rs),
        'b_w_qkv': nrm((N_B, D, 3 * D), rs),
        'b_w_o': nrm((N_B, D, D), rs),
        'b_bias': SB_BIAS_INIT + nrm((N_B, H), 0.3),
        'r7_mu': unif((N_C, 6, D), 0.0, 1.0),
        'r7_w_rkv': nrm((N_C, 3, D, D), rs),
        'r7_w0': unif((N_C, D), -3.0, 0.0),
        'r7_w1': nrm((N_C, D, DECAY_LORA), rs),
        'r7_w2': nrm((N_C, DECAY_LORA, D), 0.1 * DECAY_LORA ** -0.5),
        'r7_a0': nrm((N_C, D), 0.1),
        'r7_a1': nrm((N_C, D, AAA_LORA), rs),
        'r7_a2': nrm((N_C, AAA_LORA, D), AAA_LORA ** -0.5),
        'r7_g1': nrm((N_C, D, GATE_LORA), rs),
        'r7_g2': nrm((N_C, GATE_LORA, D), GATE_LORA ** -0.5),
        'r7_k_k': 0.85 + nrm((N_C, D), 0.05),
        'r7_k_a': 1.0 + nrm((N_C, D), 0.05),
        'r7_r_k': nrm((N_C, H, Dh), 0.1),
        'r7_ln_w': 1.0 + nrm((N_C, D), 0.02),
        'r7_ln_b': nrm((N_C, D), 0.02),
        'r7_w_o': nrm((N_C, D, D), rs),
        'f_w_gu': nrm((DEPTH, D, 2 * F), rs),
        'f_conv': nrm((DEPTH, CONV_W, F), CONV_W ** -0.5),
        'f_w_down': nrm((DEPTH, F, D), F ** -0.5),
    }

def reference(x_prompt, x_sample, cache_k, cache_v, page_table, state_conv_a, state_wkv,
              state_shift, state_ffn_conv, c_prompt, c_sample, ada_w, ada_b, norm_g,
              a_w_in, a_conv, a_w_out, b_w_qkv, b_w_o, b_bias, r7_mu, r7_w_rkv, r7_w0, r7_w1,
              r7_w2, r7_a0, r7_a1, r7_a2, r7_g1, r7_g2, r7_k_k, r7_k_a, r7_r_k, r7_ln_w, r7_ln_b,
              r7_w_o, f_w_gu, f_conv, f_w_down):
    prm = dict(ada_w=ada_w, ada_b=ada_b, norm_g=norm_g, a_w_in=a_w_in, a_conv=a_conv,
               a_w_out=a_w_out, b_w_qkv=b_w_qkv, b_w_o=b_w_o, b_bias=b_bias, r7_mu=r7_mu,
               r7_w_rkv=r7_w_rkv, r7_w0=r7_w0, r7_w1=r7_w1, r7_w2=r7_w2, r7_a0=r7_a0,
               r7_a1=r7_a1, r7_a2=r7_a2, r7_g1=r7_g1, r7_g2=r7_g2, r7_k_k=r7_k_k,
               r7_k_a=r7_k_a, r7_r_k=r7_r_k, r7_ln_w=r7_ln_w, r7_ln_b=r7_ln_b, r7_w_o=r7_w_o,
               f_w_gu=f_w_gu, f_conv=f_conv, f_w_down=f_w_down)
    Bp = x_prompt.shape[0]
    dt = x_prompt.dtype
    z_conv_a = jnp.zeros((N_A, Bp, CONV_W - 1, D_MODEL), dt)
    z_wkv = jnp.zeros((N_C, Bp, N_HEADS, HEAD_DIM, HEAD_DIM), dt)
    z_shift = jnp.zeros((N_C, Bp, D_MODEL), dt)
    z_ffn = jnp.zeros((DEPTH, Bp, CONV_W - 1, D_FF), dt)
    y_p, ca_p, k_p, v_p, wkv_p, sh_p, ff_p = trunk(
        x_prompt, c_prompt, z_conv_a, None, None, None, z_wkv, z_shift, z_ffn, prm)
    y_s, ca_s, k_s, v_s, wkv_s, sh_s, ff_s = trunk(
        x_sample, c_sample, state_conv_a, cache_k, cache_v, page_table, state_wkv,
        state_shift, state_ffn_conv, prm)
    return (y_p, y_s, k_p, v_p, k_s, v_s, ca_p, ca_s, wkv_p, wkv_s, sh_p, sh_s, ff_p, ff_s)


_drawn_inputs = setup_inputs


def setup_inputs(seed=0):
    import zlib

    import numpy as np

    out = dict(_drawn_inputs(seed))
    spreads = {}
    factors = {'r7_w1': 3.658, 'r7_w2': 2.775, 'r7_ln_w': 8.0, 'r7_ln_b': 8.0}
    for name, (base, spread) in spreads.items():
        noise = np.random.default_rng([zlib.crc32(name.encode()), seed]).standard_normal(out[name].shape)
        drawn = base * np.exp(spread * noise) if base else spread * noise
        out[name] = __import__('jax').numpy.asarray(drawn.astype(out[name].dtype))
    for name, factor in factors.items():
        out[name] = (out[name] * factor).astype(out[name].dtype)
    return out
```

```python
import concourse.bass as bass
from concourse import mybir
import math
from contextlib import ExitStack

F32 = mybir.dt.float32
F32R = mybir.dt.float32r
I32 = mybir.dt.int32
ALU = mybir.AluOpType
ACT = mybir.ActivationFunctionType
P = 128

D = 1024
KT = D // P
NP_TOK = 512
NB, NT = 8, 8
NS_TOK = NB * NT
T = NP_TOK + NS_TOK
TH = T // 2
DEPTH = 4
F = 2816
FT = F // P
NSEQ = 1 + NB
HD = 64
NH = D // HD
HIST = 2
PADW = HIST + NP_TOK + NB * (NT + HIST)
CW = PADW - HIST
SROW = HIST + NP_TOK
PAGE, NPAGE = 128, 2
EPS = 1e-6
GN_EPS = 64e-5
DECAY = math.exp(-0.5)

R_NORM, R_CONVA, R_MU, R_W0, R_A0, R_KK, R_KA, R_RK, R_LNW, R_LNB = 0, 16, 22, 28, 29, 30, 31, 32, 33, 34
R_ADAB, R_C, R_STA, R_SSH, R_END = 35, 59, 68, 100, 108


class At:

    def __init__(self, base, i=None, step=0):
        self.base, self.i, self.step = base, i, 0 if i is None else step

    def __add__(self, k):
        return At(self.base + k, self.i, self.step)

    def mod(self, q):
        assert self.step % q == 0
        return self.base % q

    def div(self, q):
        assert self.step % q == 0
        return At(self.base // q, self.i, self.step // q)

    def value(self):
        return self.base if self.i is None or not self.step else self.i * self.step + self.base


def due(n):
    return (n.base if isinstance(n, At) else n) >= 1


def count_of(n):
    if not isinstance(n, At):
        return n
    assert n.base >= 1, "a loop's first turn must not wait below one"
    return n.value()


def turns(eng, n, body):
    if n == 1:
        body(None)
    elif n > 1:
        with eng.Fori(0, n) as i:
            body(i)


def par_rows(x):
    return [
        (R_NORM, x["norm_g"].rearrange("l n d -> (l n) d")),
        (R_CONVA, x["a_conv"].rearrange("j w d -> (j w) d")),
        (R_MU, x["r7_mu"][0]),
        (R_W0, x["r7_w0"]), (R_A0, x["r7_a0"]), (R_KK, x["r7_k_k"]), (R_KA, x["r7_k_a"]),
        (R_RK, x["r7_r_k"].rearrange("j h d -> j (h d)")), (R_LNW, x["r7_ln_w"]), (R_LNB, x["r7_ln_b"]),
        (R_ADAB, x["ada_b"].rearrange("l (m d) -> (l m) d", m=6)),
        (R_C, x["c_prompt"]), (R_C + 1, x["c_sample"]),
        (R_STA, x["state_conv_a"].rearrange("j b r d -> (j b r) d")),
        (R_SSH, x["state_shift"][0]),
    ]


def trunk_program(nc, x, o, depth=DEPTH):
    ctx = ExitStack()
    with ctx:
        place = [(nc.sbuf_base + 31) // 32 * 32]
        place_of = {}

        def room(size):
            at = place[0]
            place[0] += (size + 31) // 32 * 32
            return at

        def sb(name, shape, dt=F32, at=None):
            size = 4
            for s in shape[1:]:
                size *= s
            at = room(size) if at is None else at
            assert at + size <= nc.sbuf_usable_end, name
            place_of[name] = at
            return nc.alloc_sbuf_tensor_at(name, shape, dt, offset=at)

        ROW = 4 * T
        X = sb("X", [P, KT, T])
        u_at = room(2 * KT * ROW)
        h_at = room(2 * FT * ROW)
        h_end = h_at + 2 * FT * ROW
        Uh = sb("Uh", [P, KT, T], F32R, u_at)
        Ul = sb("Ul", [P, KT, T], F32R, u_at + KT * ROW)
        Uf = sb("Uf", [P, KT, T], F32, u_at + KT * ROW)
        O = sb("O", [P, KT, T], F32, u_at)
        Hh = sb("Hh", [P, FT, T], F32R, h_at)
        Hl = sb("Hl", [P, FT, T], F32R, h_at + FT * ROW)
        Hf = sb("Hf", [P, FT, T], F32, h_at + FT * ROW)
        par = sb("par", [P, D], F32, h_at)
        xrow = sb("xrow", [P, 5, D], F32, h_at + 4 * D)
        yrow = sb("yrow", [P, 5, D], F32, h_at)
        rout = sb("rout", [HIST * NSEQ, F], F32, h_at)
        srow = sb("srow", [3 + NB * HIST, F], F32, h_end - 4 * F)
        MR = sb("MR", [NSEQ, 24, P], F32, h_at + 16 * F)
        raw = sb("raw", [P, 4, KT, P])
        SH = sb("SH", [P, 2, KT, P], F32R)
        SL = sb("SL", [P, 2, KT, P], F32R)
        gp_at = room(8 * PADW)
        GP = sb("GP", [P, 2, PADW], F32, gp_at)
        SQ = sb("SQ", [P, 2, T], F32, gp_at)
        cv_at = room(4 * PADW)
        CV = sb("CV", [P, PADW], F32, cv_at)
        RS = sb("RS", [P, T], F32, cv_at)
        slc_at = room(ROW)
        SLC = sb("SLC", [P, T], F32, slc_at)
        T1 = sb("T1", [P, T], F32, slc_at)
        MOD = sb("MOD", [P, 3, 3, KT, NSEQ])
        PT = sb("PT", [P, KT, R_END])
        CT = sb("CT", [P, KT, NSEQ])
        ST = sb("ST", [P, FT, 3 + NB * HIST])
        TL = sb("TL", [P, FT, HIST * NSEQ])
        ident = sb("ident", [P, P])
        ones = sb("ones", [P, P])
        ntri = sb("ntri", [P, P])
        nones = sb("nones", [P, P])
        BB = sb("BB", [P, NH])
        pages = sb("pages", [1, NB * NPAGE], I32)

        S = KT * ROW
        QF = sb("QF", [P, KT, T], F32, h_at)
        KF = sb("KF", [P, KT, T], F32, h_at + S)
        VF = sb("VF", [P, KT, T], F32, h_at + 15 * S // 4)
        VT = sb("VT", [P, 5, D], F32, u_at)
        KR = sb("KR", [P, 4, D], F32, u_at + 20 * D)
        KS = sb("KS", [NS_TOK, D], F32, h_at + 19 * S // 4)
        w1_at, w2_at, w3_at = u_at + 20 * D, h_at + 2 * S, h_at + 19 * S // 4
        ZB = sb("ZB", [P, 2, 512], F32, w1_at)
        EX = sb("EX", [P, 2, 512], F32, w1_at + 4096)
        SP = sb("SP", [P, 2, 512], F32, w1_at + 8192)
        SUM = sb("SUM", [P, 2, 512], F32, w1_at + 12288)
        AT = sb("AT", [P, 2, 1280], F32, w2_at)
        PG = sb("PG", [P, 4, D], F32, u_at)
        SE = sb("SE", [P, 3, D], F32, w1_at)
        QB = sb("QB", [P, KT, 2, NS_TOK], F32, w1_at + 12 * D)
        SZ = sb("SZ", [P, 3, D], F32, w3_at)
        KTP = sb("KTP", [P, NPAGE, KT, P], F32, w2_at)

        XS = nc.dram_tensor("x_spill", (P, KT, T), F32, kind="Internal").ap()
        w_at = u_at + S
        Df = sb("Df", [P, KT, T], F32, u_at)
        XMh = sb("XMh", [P, KT, T], F32R, h_at)
        XMl = sb("XMl", [P, KT, T], F32R, h_at + S)
        XMf = sb("XMf", [P, KT, T], F32, h_at + S)
        A_ = sb("A_", [P, KT, T], F32, h_at + 2 * S)
        B_ = sb("B_", [P, KT, T], F32, h_at + 3 * S)
        K_ = sb("K_", [P, KT, T], F32, h_at + 4 * S)
        R_ = sb("R_", [P, KT, T], F32, place_of["X"])
        V_ = sb("V_", [P, KT, T], F32, u_at)
        GHh = sb("GHh", [P, 2, T], F32R, h_at + 5 * S)
        GHl = sb("GHl", [P, 2, T], F32R, h_at + 5 * S + 2 * ROW)
        GHf = sb("GHf", [P, 2, T], F32, h_at + 5 * S + 2 * ROW)
        HDh = sb("HDh", [P, T], F32R, gp_at)
        HDl = sb("HDl", [P, T], F32R, gp_at + ROW)
        HDf = sb("HDf", [P, T], F32, gp_at + ROW)
        DQ = sb("DQ", [P, 2, T], F32, h_at)
        DR = sb("DR", [P, 2, T], F32, h_at + 2 * ROW)
        DK = sb("DK", [P, 2, T], F32, h_at + 4 * ROW)
        IB = sb("IB", [P, 2, T], F32, h_at + 6 * ROW)
        PB = sb("PB", [P, 2, T], F32, h_at + 8 * ROW)
        SHR = sb("SHR", [NSEQ, D], F32, h_at + 4 * S)
        c_at = [w_at]

        def keeps(name, shape, at=c_at):
            size = 4
            for d in shape[1:]:
                size *= d
            out = sb(name, shape, F32, at[0])
            at[0] += (size + 31) // 32 * 32
            return out

        M2 = keeps("M2", [P, 2, 2, P])
        LM = keeps("LM", [P, 6, P])
        SAME = keeps("SAME", [P, 7, P])
        SF = keeps("SF", [P, KT, HD])
        RM = keeps("RM", [P, T])
        J2 = keeps("J2", [P, HD])
        ZERO = keeps("ZERO", [P, HD])
        PC = keeps("PC", [P, KT, 16])
        MKA = keeps("MKA", [P, KT])
        assert c_at[0] <= w_at + S
        BO = SAME[:, 6, :]

        class Unit:

            def __init__(w, tag, at, n, levels, bank, group=0):
                w.n, w.levels, w.bank, w.group, w.prompt = n, levels, bank, group, n == P
                mk = lambda name, *shape: keeps(name + tag, list(shape), at)
                w.FS = mk("FS", P, 5, n)
                w.TM = mk("TM", n, 4, P)
                w.MM = mk("MM", n, 2, 2, 2, n)
                w.ML = mk("ML", n, 2, 2, n)
                w.TB = mk("TB", n, 2, 2, n)
                w.AB = mk("AB", n, 2, n)
                w.NV = mk("NV", n, 2, HD)
                w.UW = mk("UW", n, 2, 2, HD)
                w.RP = mk("RP", P, n)
                if w.prompt:
                    w.GG = mk("GG", P, 2, HD)
                    w.SC = mk("SC", P, HD)
                else:
                    w.GG = mk("GG", P, NB, HD)
                    w.SN = mk("SN", HD, NB, P)
                    w.S0 = mk("S0", P, NB, HD)
                    w.S1 = mk("S1", P, NB, HD)
                    w.BM = mk("BM", n, 2, NB, HD)
                    w.UM = mk("UM", n, 2, NB, HD)
                    w.VM = mk("VM", n, 2, NB, HD)

        wp_at, ws_at = [h_at], [h_at]
        WP = [Unit(f"p{g}", wp_at, P, 6, 4 * g, g) for g in range(2)]
        WS = Unit("s", ws_at, NS_TOK, 3, 0)
        assert wp_at[0] <= h_at + 2 * S and ws_at[0] <= h_at + 2 * S - 4 * D
        SO = sb("SO", [HD, KT, P], F32, h_at + 2 * S - 4 * D)

        ps = ctx.enter_context(nc.psum_tensor("ps", [P, 8, 512], F32))
        ADA, SS, TR = 4, 5, 7

        def sem(name):
            return ctx.enter_context(nc.semaphore(name))

        raw_full = [sem(f"raw_full{r}") for r in range(4)]
        hi_done, lo_done = sem("hi_done"), sem("lo_done")
        main_used, ada_used = sem("main_used"), sem("ada_used")
        tile_free = [sem("tile_free0"), sem("tile_free1")]
        sq_ready, sq_used, ss_read, root_done = sem("sq_ready"), sem("sq_used"), sem("ss_read"), sem("root_done")
        x_ready, uf_ready, uh_ready, u_ready = sem("x_ready"), sem("uf_ready"), sem("uh_ready"), sem("u_ready")
        mod_ready, mr_ready, ada_turned = sem("mod_ready"), sem("mr_ready"), sem("ada_turned")
        hh_ready, mix_ready, cv_seq, silu_ready = sem("hh_ready"), sem("mix_ready"), sem("cv_seq"), sem("silu_ready")
        pad_ready, tail_ready = sem("pad_ready"), sem("tail_ready")
        tr_full, tr_free = sem("tr_full"), sem("tr_free")
        par_in, x_in, rows_in, rows_out = sem("par_in"), sem("x_in"), sem("rows_in"), sem("rows_out")
        const_ready = sem("const_ready")
        dve_seq, pool_seq, act_seq = sem("dve_seq"), sem("pool_seq"), sem("act_seq")
        (z_ready, zb_ready, abs_ready, ln_ready, sp_ready, spm_ready, sum_ready, cum_done, a_ready, am_ready,
         av_done, av_read) = (sem(f"at_{n}") for n in
                              ("z_ready", "zb_ready", "abs_ready", "ln_ready", "sp_ready", "spm_ready", "sum_ready",
                               "cum_done", "a_ready", "am_ready", "av_done", "av_read"))
        xd_ready, xf_ready, xh_ready, xm_ready = (sem(f"r_{n}") for n in ("d_ready", "f_ready", "h_ready", "m_ready"))
        ur_ready, lr_tile, hd_ready, hd_split, spilled, x_back, shift_out, wkv_out = (sem(n) for n in
            ("ur_ready", "lr_tile", "hd_ready", "hd_split", "spilled", "x_back", "shift_out", "wkv_out"))
        mask_ready = sem("mask_ready")
        bs_in, bs_out, bs_read, bs_in2, bs_rooted = (sem(n) for n in
            ("bs_in", "bs_out", "bs_read", "bs_in2", "bs_rooted"))
        scanned, grown = sem("scanned"), sem("grown")
        kv_out, misc_in, pages_used = sem("kv_out"), sem("misc_in"), sem("pages_used")
        page_full = [sem(f"page_full{r}") for r in range(4)]
        kt_full, kt_free, kt_used = sem("kt_full"), sem("kt_free"), sem("kt_used")
        (szr, szb, sabs, sln, ssp, sspm, scum, sw, sa, sam, sav, sav_read) = (sem(f"s_{n}") for n in
            ("z_ready", "zb_ready", "abs_ready", "ln_ready", "sp_ready", "spm_ready", "cum_done", "w_ready",
             "a_ready", "am_ready", "av_done", "av_read"))

        class UnitSems:

            def __init__(q, tag):
                q.free, q.staged = sem(tag + "free"), sem(tag + "staged")
                q.prod, q.turned = sem(tag + "prod"), sem(tag + "turned")
                q.mm, q.ml = sem(tag + "mm"), sem(tag + "ml")
                q.lva, q.lvt, q.inv = sem(tag + "lva"), sem(tag + "lvt"), sem(tag + "inv")
                q.nv_out, q.uw_out = sem(tag + "nv_out"), sem(tag + "uw_out")
                q.copied = sem(tag + "copied")
                q.umask, q.rgh, q.rp = sem(tag + "umask"), sem(tag + "rgh"), sem(tag + "rp")
                q.chain, q.state, q.y = sem(tag + "chain"), sem(tag + "state"), sem(tag + "y")

        QP, QS = [UnitSems("wkvp0_"), UnitSems("wkvp1_")], UnitSems("wkvs_")
        sn_in, s0_out, s0_in, s1_out, sn_back = (sem(n) for n in ("sn_in", "s0_out", "s0_in", "s1_out", "sn_back"))
        sf_out, so_ready, settled = sem("sf_out"), sem("so_ready"), sem("settled")

        def settle(eng):
            eng.sem_inc(settled, 1)

        def prompt_units(eng, unit, start=None):
            with eng.Fori(0, KT // 2) as pp:
                for g in range(2):
                    if start:
                        start(g, pp)
                with eng.Fori(0, NP_TOK // P) as b:
                    units = [unit(WP[g], QP[g], pp * (NP_TOK // P) + b, pp * 2 + g, b) for g in range(2)]
                    for _ in zip(*units):
                        pass

        def sample_units(eng, unit):
            with eng.Fori(0, KT) as p:
                for _ in unit(WS, QS, p, p, None):
                    pass

        def of_unit(a, w, pair, b):
            cols = bass.ds(b * P, P) if w.prompt else slice(NP_TOK, T)
            return a[:, bass.ds(pair, 1), cols].rearrange("p a t -> p (a t)")

        def chunk_end(pair, b, c):
            return PC[:, bass.ds(pair, 1), bass.ds(b * 2 + c, 1)].rearrange("p a c -> p (a c)")

        halves_of = lambda a: a.rearrange("p (h t) -> p h t", h=2)

        def tile_ps(t):
            return ps[:, 2 * t.mod(2):2 * t.mod(2) + 2, 0:TH]

        def pieces(t):
            b = 2 * t.mod(2)
            return (ps[:, b, 0:TH], ps[:, b + 1, 0:NP_TOK - TH],
                    ps[:, b + 1, NP_TOK - TH:TH].rearrange("p (s t) -> p s t", s=NB))

        seqs = lambda a: a.rearrange("p (s t) -> p s t", s=NB)

        def padded(row):
            return (row[:, HIST:HIST + TH], row[:, HIST + TH:HIST + NP_TOK],
                    seqs(row[:, SROW:PADW])[:, :, HIST:HIST + NT])

        def convolved(row):
            return (row[:, 0:TH], row[:, TH:NP_TOK], seqs(row[:, SROW:PADW])[:, :, 0:NT])

        kp = lambda w: w.rearrange("(k p) e -> p k e", p=P)

        def col(w, c):
            return w[:, :, bass.ds(c * P, P)]

        DOWN = ((0, 8), (8, 15), (15, FT))

        class Stage:

            def __init__(s, name, layer, n, body, src, per_tile=1, halves=(), tiles=None):
                s.name, s.layer, s.n, s.body, s.src, s.per_tile, s.halves = name, layer, n, body, src, per_tile, halves
                s.tiles = tiles or n * body // per_tile

            def slot(s, c, i):
                first = 24 * len(s.halves) if (i is not None or c >= 2) else 0
                return At(s.m0 + c, i, s.body), At(s.n0 + c + first, i, s.body)

        def stages_of(l):
            kind, j = l % 3, l // 3
            half = (2 * l + 1,) if l else ()
            if kind == 0:
                w, wo = kp(x["a_w_in"][j]), kp(x["a_w_out"][j])
                yield Stage("in", l, 2, 12, lambda c, i: col(w, i * 4 + (c // 3 + (8, 16, 0)[c % 3])), halves=half)
            elif kind == 1:
                w, wo = kp(x["b_w_qkv"][j]), kp(x["b_w_o"][j])
                yield Stage("qkv", l, 3, 8, lambda c, i: col(w, i * 8 + c), halves=half)
            else:
                wo = kp(x["r7_w_o"][j])
                rkv = [kp(x["r7_w_rkv"][j][q]) for q in range(3)]
                lanes = lambda a: a.rearrange("p (k e) -> p k e", e=P)
                g1 = kp(x["r7_g1"][j])
                srcs = [kp(x["r7_w1"][j]), lanes(x["r7_w2"][j]), kp(x["r7_a1"][j]), lanes(x["r7_a2"][j])]
                srcs += [rkv[q][:, :, e * P:(e + 1) * P] for q in (1, 0) for e in range(KT)]
                srcs += [g1[:, :, 0:P], g1[:, :, P:]]
                srcs += [rkv[2][:, :, e * P:(e + 1) * P] for e in range(KT)]
                yield Stage("rwkv", l, 1, len(srcs), lambda c, i: srcs[c], halves=half, tiles=44)
                g2 = x["r7_g2"][j]
                yield Stage("g2", l, 1, 2, lambda c, i: lanes(g2[c * P:min(c * P + P, g2.shape[0])]), tiles=KT)
            yield Stage("out", l, 2, 4, lambda c, i: col(wo, i * 4 + c))
            gu, wd = kp(x["f_w_gu"][l]), kp(x["f_w_down"][l])
            yield Stage("gu", l, 11, 4, lambda c, i: col(gu, i * 2 + (c // 2 + FT * (c % 2))),
                        halves=(2 * l + 2,) if l + 1 < depth else ())
            yield Stage("down", l, 2, 12, lambda c, i: col(wd[:, slice(*DOWN[c % 3])], i * 4 + c // 3), per_tile=3)

        plan = [s for l in range(depth) for s in stages_of(l)]
        m = t = cv = mix = 0
        n = 48
        for s in plan:
            s.m0, s.t0, s.n0, s.cv0, s.mix0 = m, t, n, cv, mix
            m += s.n * s.body
            t += s.tiles
            n += s.n * s.body + 24 * len(s.halves)
            cv += {"in": KT, "gu": FT}.get(s.name, 0)
            mix += {"in": KT, "gu": FT, "qkv": KT, "g2": KT}.get(s.name, 0)
            s.m1, s.t1, s.cv1, s.mix1 = m, t, cv, mix
        SLOTS = m

        def run(eng, s, step, per_turn=None):
            per_turn = per_turn or s.body
            if s.m0 == 0:
                for c in range(s.n * per_turn):
                    step(c, None)
            else:
                def body(i):
                    for c in range(per_turn):
                        step(c, i)
                turns(eng, s.n, body)

        W1, W2, A1, A2, KP, RP_, G1, VP = range(8)
        LANES = ((3, 1, 0), (None, 1, 1), (4, 1, 9), (None, 1, 10), (1, KT, 18), (0, KT, 26), (5, 2, 34), (2, KT, 36))

        def lanes():
            c = 0
            for path, (mu, n, t) in enumerate(LANES):
                for j in range(n):
                    yield path, c, j, mu if j == 0 else None, t + j
                    c += 1

        SQUARES = (4, 6, 8, 9, 11, 13, 14, 16)
        TAKEN = (1, 3, 5, 7)

        block = ctx.enter_context(nc.Block())

        @block.sync
        def _(sp):
            ada_n = [0]

            def load(n, src):
                sp.dma_start(raw[0:src.shape[0], n.mod(4), 0:src.shape[1], 0:src.shape[2]], src).then_inc(raw_full[n.mod(4)], 16)

            def load_ada(n, half, k):
                w = kp(x["ada_w"][half // 2])
                load(n, col(w, half % 2 * 24 + k))
                ada_n[0] += 1

            for k in range(48):
                if due(k - 3):
                    sp.wait_ge(ada_used, k - 3)
                load_ada(At(k), k // 24, k % 24)
            sp.wait_ge(ada_used, 48)

            for s in plan:
                for c in range(2):
                    m, n = s.slot(c, None)
                    if due(m + (-3)):
                        sp.wait_ge(lo_done, count_of(m + (-3)))
                    load(n, s.src(c, 0))
                for half in s.halves:
                    for k in range(24):
                        if k < 4:
                            sp.wait_ge(lo_done, s.m0 - 1 + k)
                        else:
                            sp.wait_ge(ada_used, ada_n[0] - 3)
                        load_ada(At(s.n0 + 2 + k), half, k)
                    sp.wait_ge(ada_used, ada_n[0])

                def shifted(i, s=s):
                    for c in range(2, s.body + 2):
                        m, n = At(s.m0 + c, i, s.body), At(s.n0 + c + 24 * len(s.halves), i, s.body)
                        if due(m + (-3)):
                            sp.wait_ge(lo_done, count_of(m + (-3)))
                        load(n, s.src(c % s.body, (0 if i is None else i) + c // s.body))
                turns(sp, s.n - 1, shifted)
                for c in range(2, s.body):
                    c += (s.n - 1) * s.body
                    m, n = s.slot(c, None)
                    sp.wait_ge(lo_done, count_of(m + (-3)))
                    load(n, s.src(c % s.body, c // s.body))

        @block.tensor
        def _(pe):
            count = dict(sq=0, ada=0, half=0, tr=0, u=0)

            def tile(s, c, i, hi, lo, parts, ready):
                t = At(s.t0 + c, i, s.body // s.per_tile)
                b = 2 * t.mod(2)
                if due(t.div(2)):
                    pe.wait_ge(tile_free[t.mod(2)], count_of(t.div(2)))
                for q, (k0, k1) in enumerate(parts):
                    m = At(s.m0 + c * len(parts) + q, i, s.body)
                    pe.wait_ge(lo_done, count_of(m + 1))
                    for k in range(k0, k1):
                        ready(k)
                        wh, wl = SH[:, m.mod(2), k - k0, :], SL[:, m.mod(2), k - k0, :]
                        last = k == k1 - 1 and q == len(parts) - 1
                        for w, a, on, off in ((wh, hi, k == 0, False), (wh, lo, False, False), (wl, hi, False, last)):
                            for h in range(2):
                                mm = pe.matmul(ps[:, b + h, 0:TH], w, a[:, k, h * TH:(h + 1) * TH], start=on, stop=off)
                    mm.then_inc(main_used, 1)

            def sum_squares(k):
                n = count["sq"]
                if k == 0:
                    if due(n // KT):
                        pe.wait_ge(ss_read, n // KT)
                pe.wait_ge(sq_ready, n + 1)
                for h in range(2):
                    mm = pe.matmul(ps[:, SS + h, 0:TH], ones[:], SQ[:, n % 2, h * TH:(h + 1) * TH],
                                   start=(k == 0), stop=(k == KT - 1))
                mm.then_inc(sq_used, 1)
                count["sq"] = n + 1

            def modulation(k, free=0):
                n, r, group = count["ada"], count["raw"], k // 4
                pe.wait_ge(raw_full[r % 4], 16 * (r // 4 + 1))
                if group < 2 and k % 4 == 0 and free:
                    pe.wait_ge(tile_free[0], free)
                    pe.wait_ge(tile_free[1], free)
                if group >= 4:
                    pe.wait_ge(mr_ready, 6 * (n // 24) + group - 3)
                for q in range(KT):
                    mm = pe.matmul(ps[0:NSEQ, group % 4, k % 4 * P:k % 4 * P + P], CT[:, q, :], raw[:, r % 4, q, :],
                                   start=(q == 0 and k % 4 == 0), stop=(q == KT - 1), skip_group_check=True)
                mm.then_inc(ada_used, 1)
                count["ada"], count["raw"] = n + 1, r + 1

            def turn_modulations():
                pe.wait_ge(mr_ready, count["ada"] // 4)
                if count["half"]:
                    pe.wait_ge(mod_ready, count["half"])
                for k in range(24):
                    mm = pe.transpose(ps[:, ADA, k * NSEQ:(k + 1) * NSEQ], MR[:, k, :], ident[0:NSEQ, 0:NSEQ])
                mm.then_inc(ada_turned, 1)
                count["half"] += 1

            def transposes(srcs, rows, cols, width, bank=TR, behind=0):
                if due(count["tr"] - behind):
                    pe.wait_ge(tr_free, count["tr"] - behind)
                for g, a in enumerate(srcs):
                    mm = pe.transpose(ps[0:cols, bank, g * width:g * width + rows], a, ident[0:rows, 0:rows])
                mm.then_inc(tr_full, 1)
                count["tr"] += 1

            def attention(s):
                pe.wait_ge(tile_free[0], s.t1 // 2)
                pe.wait_ge(tile_free[1], s.t1 // 2)
                pe.wait_ge(tr_free, count["tr"])
                for a in (VF, KF):
                    for g in range(4):
                        for hh in range(2):
                            transposes([a[:, 4 * hh + q, g * P:(g + 1) * P] for q in range(4)], P, P, P,
                                       (TR, TR - 1)[hh], 1)
                    for hh in range(2):
                        transposes([a[:, 4 * hh + q, NP_TOK:T] for q in range(4)], P, NS_TOK, P, (TR, TR - 1)[hh], 1)
                pe.wait_ge(tr_free, count["tr"])

                def where(pc):
                    return pc // 4, 3 - pc % 4

                def scores(pc):
                    h, kb = where(pc)
                    r, w = 64 * (h % 2), NP_TOK - kb * P
                    if due(pc - 3):
                        pe.wait_ge(a_ready, pc - 3)
                    pe.matmul(ps[:, pc % 4, 0:w], KF[r:r + HD, h // 2, kb * P:(kb + 1) * P],
                              QF[r:r + HD, h // 2, kb * P:NP_TOK], start=True, stop=True).then_inc(z_ready, 1)

                def cumulate(pc):
                    h, kb = where(pc)
                    w = NP_TOK - kb * P
                    pe.wait_ge(spm_ready, pc + 1)
                    mm = pe.matmul(ps[:, pc % 4, 0:w], ntri[:], SP[:, pc % 2, 0:w], start=False, stop=True,
                                   skip_group_check=True)
                    if kb < 3:
                        pe.wait_ge(sum_ready, pc)
                        mm = pe.matmul(ps[:, pc % 4, P:w], nones[:], SUM[:, (pc - 1) % 2, 0:w - P],
                                       start=False, stop=True, skip_group_check=True)
                    mm.then_inc(cum_done, 1)

                def values(h):
                    r, b = 64 * (h % 2), 4 + h // 2 % 2
                    pe.wait_ge(am_ready, 4 * h + 4)
                    if due(h // 2 - 1):
                        pe.wait_ge(av_read, h // 2 - 1)
                    at = AT[:, h % 2, :]
                    for kb in range(4):
                        o0 = (0, P, 3 * P, 6 * P)[3 - kb]
                        w = NP_TOK - kb * P
                        mm = pe.matmul(ps[r:r + HD, b, kb * P:NP_TOK], VT[:, kb, h * HD:(h + 1) * HD],
                                       at[:, o0:o0 + w], start=(kb == 0), stop=(kb == 3))
                    mm.then_inc(av_done, 1)

                for k in range(4 * NH + 5):
                    if k < 4 * NH:
                        scores(k)
                    if 2 <= k < 4 * NH + 2:
                        cumulate(k - 2)
                    if k % 4 == 0 and 8 <= k:
                        values(k // 4 - 2)

                pe.wait_ge(av_read, KT + 2)
                opened = set()
                sc = lambda h: h * NS_TOK
                for k in range(KT):
                    pe.matmul(ps[0:NS_TOK, 4 + k // 4, k % 4 * P:k % 4 * P + P], KF[:, k, NP_TOK:T],
                              QB[:, k].rearrange("p r c -> p (r c)"), start=(k % 4 == 0), stop=True,
                              skip_group_check=True)
                g = 0
                for b in range(NB):
                    for j in range(NPAGE):
                        n = NPAGE * b + j
                        pe.wait_ge(page_full[n % 4], 16 * (n // 4 + 1))
                        for hh in range(2):
                            if due(g - 1):
                                pe.wait_ge(kt_free, g - 1)
                            for q in range(4):
                                k = 4 * hh + q
                                mm = pe.transpose(ps[:, 6 + g % 2, q * P:(q + 1) * P], PG[:, n % 4, k * P:(k + 1) * P], ident[:])
                            mm.then_inc(kt_full, 1)
                            g += 1
                    pe.wait_ge(kt_free, g)
                    for j in range(NPAGE):
                        for k in range(KT):
                            bank, cols = 2 * j + k // 4, slice(b * NT, b * NT + NT)
                            out = ps[:, bank, k % 4 * P:k % 4 * P + P].rearrange("p (r c) -> p r c", r=2)
                            mm = pe.matmul(out[:, :, cols], KTP[:, j, k, :], QB[:, k, :, cols],
                                           start=(bank not in opened), stop=True, skip_group_check=True)
                            opened.add(bank)
                    mm.then_inc(kt_used, 1)
                for q in (2, 1, 0):
                    rows = NS_TOK if q == 2 else P
                    for hh in range(2):
                        out = ps[0:rows, (4, 2, 0)[2 - q] + hh, :]
                        cols = slice(512 * hh, 512 * hh + 512)
                        pe.wait_ge(sspm, 3 - q)
                        mm = pe.matmul(out, ntri[0:rows, 0:rows], SZ[0:rows, q, cols], start=False, stop=True,
                                       skip_group_check=True)
                        if q < 2:
                            mm = pe.matmul(out, nones[0:NS_TOK, :], SZ[0:NS_TOK, 2, cols], start=False, stop=True,
                                           skip_group_check=True)
                        if q == 0:
                            mm = pe.matmul(out, nones[:], SZ[:, 1, cols], start=False, stop=True, skip_group_check=True)
                    mm.then_inc(scum, 1)
                pe.wait_ge(kt_free, g)
                for h in range(NH):
                    r, c = 64 * (h % 2), h // 2 * NS_TOK
                    pe.wait_ge(sam, 1)
                    pe.matmul(ps[r:r + HD, 6, c:c + NS_TOK], VT[0:NS_TOK, 4, h * HD:(h + 1) * HD],
                              SE[0:NS_TOK, 2, sc(h):sc(h) + 64], start=(h < 2), stop=True, skip_group_check=True)
                pe.wait_ge(sam, 3)
                for b in range(NB):
                    for j in range(NPAGE):
                        n = NPAGE * NB + NPAGE * b + j
                        pe.wait_ge(page_full[n % 4], 16 * (n // 4 + 1))
                        for h in range(NH):
                            r, c = 64 * (h % 2), h // 2 * NS_TOK + b * NT
                            mm = pe.matmul(ps[r:r + HD, 6, c:c + NT], PG[:, n % 4, h * HD:(h + 1) * HD],
                                           SE[:, j, sc(h) + b * NT:sc(h) + (b + 1) * NT], start=False, stop=True,
                                           skip_group_check=True)
                        mm.then_inc(pages_used, 1)

            def thrice(out, start, stop, wh, wl, hi, lo, h):
                cols = slice(h * TH, (h + 1) * TH)
                pe.matmul(out, wh, hi[:, cols], start=start, stop=False)
                pe.matmul(out, wh, lo[:, cols], start=False, stop=False)
                return pe.matmul(out, wl, hi[:, cols], start=False, stop=stop)

            def low_rank(t, parts):
                pe.wait_ge(tile_free[t % 2], t // 2)
                for q, (wh, wl, hi, lo) in enumerate(parts):
                    for h in range(2):
                        mm = thrice(ps[:, 2 * (t % 2) + h, 0:TH], q == 0, q == len(parts) - 1, wh, wl, hi, lo, h)
                    yield mm

            def project(s):
                pe.wait_ge(ur_ready, KT)
                for g in range(2):
                    transposes([Uf[:, 4 * g + q, NP_TOK - 1:T:NT] for q in range(4)], P, NSEQ, P)
                mixes = splits = 0
                for path, c, j, mu, t in lanes():
                    m = s.m0 + c
                    if mu is not None:
                        mixes += 1
                    if path in (W2, A2):
                        splits += 1
                        pe.wait_ge(lo_done, m + 1)
                        pe.wait_ge(hd_split, splits)
                        for e in range(KT):
                            w = slice(0, 64), m % 2, e
                            for mm in low_rank(s.t0 + t + e, [(SH[w], SL[w], HDh[0:64], HDl[0:64])]):
                                mm.then_inc(lr_tile if e < KT - 1 else main_used, 1)
                    else:
                        ts = s.t0 + t
                        pe.wait_ge(tile_free[ts % 2], ts // 2)
                        pe.wait_ge(lo_done, m + 1)
                        for k in range(KT):
                            if j == 0:
                                pe.wait_ge(xm_ready, KT * (mixes - 1) + k + 1)
                            for h in range(2):
                                mm = thrice(ps[:, 2 * (ts % 2) + h, 0:TH], k == 0, k == KT - 1, SH[:, m % 2, k, :],
                                            SL[:, m % 2, k, :], XMh[:, k, :], XMl[:, k, :], h)
                        mm.then_inc(main_used, 1)

            def block_sum(src, ready, at):
                pe.wait_ge(ready, at)
                if due(count["bs"]):
                    pe.wait_ge(bs_read, count["bs"])
                for h in range(2):
                    mm = pe.matmul(ps[:, SS + h, 0:TH], BO, src[:, h * TH:(h + 1) * TH], start=True, stop=True)
                mm.then_inc(bs_out, 1)
                count["bs"] += 1

            def unit(w, q, i, pair, b):
                n, L, B = w.n, w.levels, w.bank
                heads = [(h, slice(HD * h, HD * h + HD)) for h in range(2)]
                mm = lambda out, l, r, start=False: pe.matmul(out, l, r, start=start, stop=True, skip_group_check=True)
                pe.wait_ge(q.staged, count_of(At(1, i, 1)))
                settle(pe)
                for h, hh in heads:
                    for kind in range(2):
                        last = mm(ps[0:n, B + h, 2 * n * kind:2 * n * kind + 2 * n].rearrange("p (x t) -> p x t", x=2),
                                  w.FS[hh, 2 + kind, :], w.FS[hh, 0:2, :], kind == 0)
                last.then_inc(q.prod, 1)
                for x, f in enumerate((0, 2, 3, 4)):
                    last = pe.transpose(ps[0:n, B + 2, x * P:x * P + P], w.FS[:, f, :], ident[:])
                last.then_inc(q.turned, 1)
                yield
                pe.wait_ge(q.mm, count_of(At(1, i, 1)))
                settle(pe)
                pe.wait_ge(q.copied, count_of(At(1, i, L + 2)))
                settle(pe)
                for h, hh in heads:
                    last = mm(ps[0:n, B + 3, HD * h:HD * h + HD], w.MM[:, h, 1, 0, :], w.TM[:, 3, hh], h == 0)
                last.then_inc(q.nv_out, 1)
                for l in range(L):
                    pe.wait_ge(q.ml, count_of(At(l + 1, i, L)))
                    settle(pe)
                    if l:
                        pe.wait_ge(q.inv, count_of(At(l, i, L)))
                        settle(pe)
                    for h, hh in heads:
                        last = mm(ps[0:n, B, n * h:n * h + n], w.ML[:, l % 2, h, :],
                                  w.TB[:, 0, h, :] if l else ident[0:n, 0:n], h == 0)
                    last.then_inc(q.lva, 1)
                    yield
                    if l:
                        pe.wait_ge(q.copied, count_of(At(2 + l, i, L + 2)))
                        settle(pe)
                        for h, hh in heads:
                            if l < L - 1:
                                mm(ps[0:n, B + 1, n * h:n * h + n], w.TB[:, 1, h, :], w.AB[:, h, :], h == 0)
                            last = mm(ps[0:n, B + 1, n * (2 + h):n * (3 + h)], w.AB[:, h, :], w.TB[:, 1, h, :],
                                      l == L - 1 and h == 0)
                        last.then_inc(q.lvt, 1)
                        yield
                pe.wait_ge(q.inv, count_of(At(L, i, L)))
                settle(pe)
                pe.wait_ge(q.copied, count_of(At(2, i, L + 2)))
                settle(pe)
                for h, hh in heads:
                    mm(ps[0:n, B, P * h:P * h + HD], w.TB[:, 1, h, :], w.NV[:, h, :], h == 0)
                    last = mm(ps[0:n, B, P * h + HD:P * h + P], w.TB[:, 1, h, :], w.TM[:, 0, hh])
                last.then_inc(q.uw_out, 1)
                if not w.prompt:
                    pe.wait_ge(sn_in, count_of(At(32, i, 32)))
                    settle(pe)
                    for e in range(NB):
                        last = pe.transpose(ps[:, 7, e * HD:(e + 1) * HD], w.SN[:, e, :], ident[0:HD, 0:HD])
                    last.then_inc(s0_out, 1)
                yield
                pe.wait_ge(q.copied, count_of(At(L + 2, i, L + 2)))
                settle(pe)
                if not w.prompt:
                    pe.wait_ge(q.umask, count_of(At(1, i, 1)))
                    settle(pe)
                for h, hh in heads:
                    rb, rk = w.MM[:, h, 0, 1, :], w.MM[:, h, 1, 1, :]
                    mm(ps[hh, B + 2, 0:n], w.UW[:, h, 1, :], rb, True)
                    mm(ps[hh, B + 2, n:2 * n], w.UW[:, h, 0, :], rb)
                    last = mm(ps[hh, B + 2, n:2 * n], w.TM[:, 3, hh], rk)
                    if not w.prompt:
                        by_seq = lambda a: a.rearrange("p s k -> p (s k)")
                        mm(ps[hh, 6, :], w.UW[:, h, 1, :], by_seq(w.BM[:, h]), True)
                        mm(ps[hh, 4, :], w.TM[:, 1, hh], by_seq(w.UM[:, h]), True)
                        last = mm(ps[hh, 4, :], w.TM[:, 2, hh], by_seq(w.VM[:, h]))
                for c in range(2 if w.prompt else 0):
                    cr, bank = slice(HD * c, HD * c + HD), B + (3, 1)[c]
                    for h, hh in heads:
                        mm(ps[hh, bank, 0:HD], w.UW[cr, h, 1, :], w.TM[cr, 1, hh], True)
                        mm(ps[hh, bank, HD:P], w.TM[cr, 1, hh], w.UW[cr, h, 0, :])
                        last = mm(ps[hh, bank, HD:P], w.TM[cr, 2, hh], w.TM[cr, 3, hh])
                last.then_inc(q.rgh, 1)
                yield
                pe.wait_ge(q.rp, count_of(At(1, i, 1)))
                settle(pe)
                if w.prompt:
                    for c in range(2):
                        if c:
                            pe.wait_ge(q.state, count_of(At(1, i, 2)))
                            settle(pe)
                        for h, hh in heads:
                            mm(ps[hh, B + 2, n + HD * c:n + HD * c + HD], w.SC[hh, :], w.RP[hh, HD * c:HD * c + HD])
                            last = mm(ps[hh, B + (3, 1)[c], HD:P], w.GG[hh, c, :], w.SC[hh, :])
                        last.then_inc(q.chain, 1)
                        yield
                else:
                    pe.wait_ge(s0_in, count_of(At(1, i, 1)))
                    settle(pe)
                    for h, hh in heads:
                        for e in range(NB):
                            mm(ps[hh, B + 2, n + NT * e:n + NT * e + NT], w.S0[hh, e, :], w.RP[hh, NT * e:NT * e + NT])
                            last = mm(ps[hh, 4, HD * e:HD * e + HD], w.GG[hh, e, :], w.S0[hh, e, :])
                    last.then_inc(q.chain, 1)
                    pe.wait_ge(q.state, count_of(At(1, i, 1)))
                    settle(pe)
                    for e in range(NB):
                        last = pe.transpose(ps[0:HD, 6 + e // 4, e % 4 * P:e % 4 * P + P], w.S1[:, e, :], ident[:])
                    last.then_inc(s1_out, 1)
                    yield

            def rwkv(s):
                project(s)
                count["bs"] = 0
                for e in range(KT):
                    if e == 0:
                        pe.wait_ge(mask_ready, 1)
                    block_sum(DQ[:, e % 2, :], bs_in, e + 1)
                prompt_units(pe, unit)
                for q in QP:
                    pe.wait_ge(q.free, 17)
                    pe.wait_ge(q.y, 17)
                for e in range(KT):
                    mm = pe.transpose(ps[0:HD, 6 + e // 4, e % 4 * P:e % 4 * P + P], SF[:, e, :], ident[:])
                mm.then_inc(sf_out, 1)
                pe.wait_ge(so_ready, 1)
                sample_units(pe, unit)
                pe.wait_ge(QS.y, KT + 1)

            def gate(s):
                pe.wait_ge(sn_back, KT)
                pe.wait_ge(lo_done, s.m1)
                for e in range(KT):
                    block_sum(A_[:, e, :], bs_read, count["bs"])
                    block_sum(SQ[:, 0, :], bs_in, KT + e + 1)
                    block_sum(SQ[:, 1, :], bs_in2, e + 1)
                    parts = [(SH[0:r, (s.m0 + j) % 2, e, :], SL[0:r, (s.m0 + j) % 2, e, :], GHh[0:r, j], GHl[0:r, j])
                             for j, r in enumerate((P, 32))]
                    for j, mm in enumerate(low_rank(s.t0 + e, parts)):
                        if e == KT - 1:
                            mm.then_inc(main_used, 1)
                        elif j:
                            mm.then_inc(lr_tile, 1)

            pe.wait_ge(const_ready, 1)
            pe.wait_ge(par_in, 16 * len(par_rows(x)))
            for g in range(2):
                transposes([par[0:R_END, (4 * g + q) * P:(4 * g + q + 1) * P] for q in range(4)], R_END, P, P)
            pe.wait_ge(x_in, 32)
            for g in range(KT):
                transposes([xrow[:, q, g * P:(g + 1) * P] for q in range(4)], P, P, P)
            transposes([xrow[0:NS_TOK, 4, g * P:(g + 1) * P] for g in range(KT)], NS_TOK, P, NS_TOK)
            pe.wait_ge(silu_ready, 1)
            count["raw"] = 0
            for k in range(24):
                modulation(k)
                if k in SQUARES:
                    sum_squares(SQUARES.index(k))
            turn_modulations()
            for k in range(24):
                modulation(k)
            turn_modulations()

            for s in plan:
                if s.name in ("in", "gu", "qkv"):
                    def u_tile(c, i, s=s):
                        tile(s, c, i, Uh, Ul, ((0, KT),),
                             lambda k: pe.wait_ge(u_ready, count["u"] + k + 1) if c == 0 else None)
                    run(pe, s, u_tile)
                    count["u"] += KT
                if s.name == "qkv":
                    attention(s)
                if s.name == "rwkv":
                    rwkv(s)
                if s.name == "g2":
                    gate(s)
                if s.name in ("out", "down"):
                    hi, lo = (XMh, XMl) if s.name == "out" and s.layer % 3 == 2 else (Hh, Hl)
                    parts = ((0, KT),) if s.name == "out" else DOWN
                    tiles = s.body // s.per_tile

                    for c in range(tiles * s.n):
                        tile(s, c, None, hi, lo, parts,
                             lambda k: pe.wait_ge(mix_ready, s.mix0 - (FT if s.name == "down" else KT) + k + 1) if c == 0 else None)
                        if c:
                            sum_squares(c - 1)
                    sum_squares(KT - 1)
                    if s.name == "out":
                        if s.layer % 3 == 0:
                            pe.wait_ge(tail_ready, s.cv0)
                            for g in range(2):
                                transposes([TL[:, 4 * g + q, :] for q in range(4)], P, HIST * NSEQ, P)
                        pe.wait_ge(rows_in, 32 * (s.layer + 1))
                        transposes([srow[:, g * P:(g + 1) * P] for g in range(FT)], 3 + NB * HIST, P, 3 + NB * HIST)
                    else:
                        pe.wait_ge(tail_ready, s.cv0)
                        for g in range(0, FT, 4):
                            transposes([TL[:, q, :] for q in range(g, min(g + 4, FT))], P, HIST * NSEQ, P)
                    nxt = plan[plan.index(s) + 1] if s.m1 < SLOTS else None
                    if nxt is None:
                        pe.wait_ge(x_ready, KT * 2 * depth)
                        for g in range(4):
                            for hh in range(2):
                                transposes([X[:, 4 * hh + q, g * P:(g + 1) * P] for q in range(4)], P, P, P)
                        for hh in range(2):
                            transposes([X[:, 4 * hh + q, NP_TOK:T] for q in range(4)], P, NS_TOK, P)
                    else:
                        count["raw"] = nxt.n0 + 2
                        for k in range(24):
                            if nxt.halves:
                                modulation(k, s.t1 // 2)
                            if k in SQUARES:
                                sum_squares(SQUARES.index(k))
                        if nxt.halves:
                            turn_modulations()

        @block.scalar
        def _(act):
            count = dict(sq=0, tr=0, root=0, u=0, x=0, rows=0, ada=0)
            copy = lambda out, in_: act.activation(out, in_, ACT.Copy)

            def split_hi(m, n):
                act.wait_ge(raw_full[n.mod(4)], count_of(At(16 * (n.base // 4 + 1), n.i, 4 * n.step)))
                if due(m + (-1)):
                    act.wait_ge(main_used, count_of(m + (-1)))
                copy(SH[:, m.mod(2)], raw[:, n.mod(4)]).then_inc(hi_done, 1)

            def ahead(s, c, i):
                if i is None and s.m0 + c + 2 >= SLOTS:
                    return
                split_hi(At(s.m0 + c + 2, i, s.body), At(s.n0 + 24 * len(s.halves) + c + 2, i, s.body))

            def square(src):
                n = count["sq"]
                if due(n - 1):
                    act.wait_ge(sq_used, n - 1)
                act.activation(SQ[:, n % 2, :] if src.shape == SQ[:, 0, :].shape else halves_of(SQ[:, n % 2, :]),
                               src, ACT.Square).then_inc(sq_ready, 1)
                count["sq"] += 1

            def root():
                act.wait_ge(ss_read, count["root"] + 1)
                act.activation(RS[:], RS[:], ACT.Sqrt).then_inc(root_done, 1)
                count["root"] += 1

            def turned(out, in_):
                act.wait_ge(tr_full, count["tr"] + 1)
                copy(out, in_).then_inc(tr_free, 1)
                count["tr"] += 1

            def take_rows():
                n = count["ada"]
                act.wait_ge(ada_used, 4 * n + 4)
                if n % 6 == 0 and n:
                    act.wait_ge(ada_turned, n // 6)
                copy(MR[:, n % 6 * 4:n % 6 * 4 + 4, :], ps[0:NSEQ, n % 6 % 4, :].rearrange("p (g c) -> p g c", g=4))\
                    .then_inc(mr_ready, 1)
                count["ada"] += 1

            def pre_norm(split, mods):
                for k in range(KT):
                    act.wait_ge(x_ready, count["x"] + k + 1)
                    square(X[:, k, :])
                    if mods and k in TAKEN:
                        take_rows()
                count["x"] += KT
                root()
                if mods:
                    take_rows()
                if not split:
                    if mods:
                        take_rows()
                    return
                for k in range(KT):
                    act.wait_ge(uf_ready, count["u"] + 1)
                    copy(Uh[:, k, :], Uf[:, k, :]).then_inc(uh_ready, 1)
                    count["u"] += 1
                    if mods and k == 2:
                        take_rows()

            def attention(s):
                for a, b, c in ((VT, VT[0:NS_TOK, 4, :], 0), (KR, KS[:], 1)):
                    for g in range(4):
                        for hh in range(2):
                            turned(a[:, g, 512 * hh:512 * (hh + 1)], ps[:, (TR, TR - 1)[hh], :])
                    for hh in range(2):
                        turned(b[:, 512 * hh:512 * (hh + 1)], ps[0:NS_TOK, (TR, TR - 1)[hh], :])

                def soft(pc):
                    w = NP_TOK - (3 - pc % 4) * P
                    e = EX[:, pc % 2, 0:w]
                    act.wait_ge(abs_ready, pc + 1)
                    act.activation(e, e, ACT.Exp, scale=-1.0).then_inc(act_seq, 1)
                    act.wait_ge(act_seq, pc + 1)
                    act.activation(e, e, ACT.Ln, bias=1.0).then_inc(ln_ready, 1)

                def weights(pc):
                    h, kb = pc // 4, 3 - pc % 4
                    w, o0 = NP_TOK - kb * P, (0, P, 3 * P, 6 * P)[3 - kb]
                    act.wait_ge(cum_done, pc + 1)
                    if due(h - 1):
                        act.wait_ge(av_done, h - 1)
                    act.activation(AT[:, h % 2, o0:o0 + w], ps[:, pc % 4, 0:w], ACT.Exp, bias=BB[:, h:h + 1])\
                       .then_inc(a_ready, 1)

                act.preload_act_table_set("natural_log_exp_and_others")
                for k in range(4 * NH + 3):
                    if k >= 3:
                        weights(k - 3)
                    if k < 4 * NH:
                        soft(k)
                for g in range(4 * NB):
                    b, j, hh = g // 4, g // 2 % 2, g % 2
                    act.wait_ge(kt_full, g + 1)
                    if due(b):
                        act.wait_ge(kt_used, b)
                    copy(KTP[:, j, 4 * hh:4 * hh + 4, :], ps[:, 6 + g % 2, :].rearrange("p (g c) -> p g c", g=4))\
                        .then_inc(kt_free, 1)
                for n, q in enumerate((2, 1, 0)):
                    e = SE[0:NS_TOK if q == 2 else P, q, :]
                    act.wait_ge(sabs, n + 1)
                    act.activation(e, e, ACT.Exp, scale=-1.0).then_inc(act_seq, 1)
                    act.wait_ge(act_seq, 4 * NH + n + 1)
                    act.activation(e, e, ACT.Ln, bias=1.0).then_inc(sln, 1)
                for n, q in enumerate((2, 1, 0)):
                    e = SE[0:NS_TOK if q == 2 else P, q, :]
                    act.wait_ge(sw, n + 1)
                    act.activation(e, e, ACT.Exp).then_inc(sa, 1)
                act.wait_ge(sav_read, 1)
                for e in range(KT):
                    copy(Hh[:, e, :], Hf[:, e, :]).then_inc(hh_ready, 1)

            def mix():
                for k in range(KT):
                    n = count["xf"]
                    act.wait_ge(xf_ready, n + 1)
                    copy(XMh[:, k, :], XMf[:, k, :]).then_inc(xh_ready, 1)
                    count["xf"] += 1

            def project(s):
                count["xf"] = 0
                act.wait_ge(sq_used, count["sq"])
                act.wait_ge(rows_out, 16 * count["rows"])
                for g in range(2):
                    turned(SHR[:, 512 * g:512 * (g + 1)], ps[0:NSEQ, TR, :])
                for path, c, j, mu, t in lanes():
                    t = s.t0 + t
                    bank = lambda t, rows=P: ps[0:rows, 2 * (t % 2):2 * (t % 2) + 2, 0:TH]
                    free = tile_free[t % 2]
                    if mu is not None:
                        mix()
                    if path in (W2, A2):
                        dst, bias = (A_, R_W0) if path == W2 else (B_, R_A0)
                        for e in range(KT):
                            if e < KT - 1:
                                act.wait_ge(lr_tile, (KT - 1) * (path == A2) + e + 1)
                            else:
                                act.wait_ge(main_used, s.m0 + c + 1)
                            act.activation(halves_of(dst[:, e, :]), bank(t + e), ACT.Sigmoid,
                                           bias=PT[:, e, bias:bias + 1]).then_inc(tile_free[(t + e) % 2], 1)
                        ahead(s, c, None)
                        continue
                    ahead(s, c, None)
                    act.wait_ge(main_used, s.m0 + c + 1)
                    if path in (W1, A1):
                        act.activation(halves_of(HDf[0:64]), bank(t, 64), ACT.Tanh if path == W1 else ACT.Copy)\
                           .then_inc(free, 1)
                        act.wait_ge(free, t // 2 + 1)
                        copy(HDh[0:64], HDf[0:64]).then_inc(hd_ready, 1)
                    elif path == G1:
                        rows = 32 if j else P
                        act.activation(halves_of(GHf[0:rows, j]), bank(t, rows), ACT.Sigmoid).then_inc(free, 1)
                        act.wait_ge(free, t // 2 + 1)
                        copy(GHh[0:rows, j], GHf[0:rows, j]).then_inc(hd_ready, 1)
                    else:
                        if path == KP and j == 0:
                            act.wait_ge(shift_out, 32)
                        if path == RP_ and j == 0:
                            act.wait_ge(spilled, 16)
                        dst = {KP: K_, RP_: R_, VP: V_}[path]
                        copy(halves_of(dst[:, j, :]), bank(t)).then_inc(free, 1)

            def unit(w, q, i, pair, b):
                n, L, B = w.n, w.levels, w.bank
                act.wait_ge(q.free, count_of(At(1, i, 1)))
                act.wait_ge(q.y, count_of(At(1, i, 1)))
                settle(act)
                for k, a in enumerate((A_, R_, B_, K_, V_)):
                    ins = copy(w.FS[:, k], of_unit(a, w, pair, b))
                ins.then_inc(q.staged, 1)
                yield
                act.wait_ge(q.turned, count_of(At(1, i, 1)))
                copy(w.TM[:].rearrange("p x d -> p (x d)"), ps[0:n, B + 2, :]).then_inc(q.copied, 1)
                yield
                act.wait_ge(q.nv_out, count_of(At(1, i, 1)))
                copy(w.NV[:].rearrange("p h d -> p (h d)"), ps[0:n, B + 3, 0:P]).then_inc(q.copied, 1)
                yield
                for l in range(1, L):
                    act.wait_ge(q.lva, count_of(At(l + 1, i, L)))
                    copy(w.AB[:].rearrange("p h t -> p (h t)"), ps[0:n, B, 0:2 * n]).then_inc(q.copied, 1)
                    yield
                act.wait_ge(q.uw_out, count_of(At(1, i, 1)))
                copy(w.UW[:].rearrange("p h x d -> p (h x d)"), ps[0:n, B, 0:2 * P]).then_inc(q.copied, 1)
                if not w.prompt:
                    act.wait_ge(s0_out, count_of(At(1, i, 1)))
                    copy(w.S0[:].rearrange("p s v -> p (s v)"), ps[:, 7, :]).then_inc(s0_in, 1)
                yield
                act.wait_ge(q.chain, count_of(At(2, i, 2) if w.prompt else At(1, i, 1)))
                settle(act)
                copy(of_unit(A_, w, pair, b), ps[:, B + 2, n:2 * n]).then_inc(q.y, 1)
                if not w.prompt:
                    act.wait_ge(s1_out, count_of(At(1, i, 1)))
                    copy(w.SN[:].rearrange("p (y x) d -> p y (x d)", y=2), ps[0:HD, 6:8, :]).then_inc(sn_back, 1)
                yield

            def rwkv(s):
                project(s)
                act.wait_ge(tile_free[0], s.t1 // 2)
                act.wait_ge(tile_free[1], s.t1 // 2)

                def norm_square(e):
                    if due(e - 1):
                        act.wait_ge(bs_out, e - 1)
                    act.activation(DQ[:, e % 2, :], K_[:, e, :], ACT.Square, scale=PT[:, e, R_KK:R_KK + 1]).then_inc(bs_in, 1)

                norm_square(0)
                for e in range(KT):
                    if e < KT - 1:
                        norm_square(e + 1)
                    act.wait_ge(bs_read, e + 1)
                    act.activation(DR[:, e % 2, :], DR[:, e % 2, :], ACT.Sqrt).then_inc(bs_rooted, 1)
                    act.wait_ge(scanned, e + 1)
                    act.activation(PB[:, e % 2, :], A_[:, e, :], ACT.Exp, scale=-DECAY)
                    act.activation(IB[:, e % 2, :], A_[:, e, :], ACT.Exp, scale=DECAY).then_inc(grown, 1)
                for q in QP:
                    act.sem_inc(q.y, 1)
                prompt_units(act, unit)
                act.wait_ge(sf_out, 1)
                copy(SO[:].rearrange("p (y x) d -> p y (x d)", y=2), ps[0:HD, 6:8, :]).then_inc(so_ready, 1)
                act.sem_inc(QS.y, 1)
                sample_units(act, unit)

            def gate(s):
                for e in range(KT):
                    act.wait_ge(bs_read, KT + 3 * e + 1)
                    act.activation(SQ[:, 0, :], T1[:], ACT.Square).then_inc(bs_in, 1)
                    act.wait_ge(bs_read, KT + 3 * e + 2)
                    act.activation(RS[:], RS[:], ACT.Sqrt).then_inc(bs_rooted, 1)
                    act.wait_ge(tile_free[(s.t0 + e) % 2], (s.t0 + e) // 2 + 1)
                    copy(XMh[:, e, :], XMf[:, e, :]).then_inc(hh_ready, 1)
                for c in range(2):
                    ahead(s, c, None)

            for g in range(2):
                turned(PT[:, 4 * g:4 * g + 4, :], ps[:, TR, :].rearrange("p (g c) -> p g c", g=4)[:, :, 0:R_END])
            act.wait_ge(tr_free, 2)
            act.activation(CT[:], PT[:, :, R_C:R_C + NSEQ], ACT.Silu).then_inc(silu_ready, 1)
            for g in range(KT):
                turned(X[:, g, 0:NP_TOK], ps[:, TR, :])
            turned(X[:, :, NP_TOK:T], ps[:, TR, :].rearrange("p (g c) -> p g c", g=KT))
            act.wait_ge(tr_free, count["tr"])
            for k in range(KT):
                square(X[:, k, :])
                if k in TAKEN:
                    take_rows()
            for g in range(2):
                take_rows()
            root()
            for k in range(KT):
                act.wait_ge(uf_ready, k + 1)
                copy(Uh[:, k, :], Uf[:, k, :]).then_inc(uh_ready, 1)
            count["u"] = KT
            for g in range(6):
                take_rows()
            for c in range(2):
                split_hi(*plan[0].slot(c, None))

            for s in plan:
                if s.name in ("in", "gu"):
                    act.wait_ge(sq_used, count["sq"])
                    if due(16 * count["rows"]):
                        act.wait_ge(rows_out, 16 * count["rows"])
                if s.name == "in":
                    def step(c, i, s=s):
                        ahead(s, c, i)
                        t = At(s.t0 + c, i, s.body)
                        if c % 3 == 0:
                            act.wait_ge(main_used, count_of(At(s.m0 + c + 1, i, s.body)))
                            if due(At(3 * (s.cv0 + c // 3), i, 12)):
                                act.wait_ge(cv_seq, count_of(At(3 * (s.cv0 + c // 3), i, 12)))
                            copy(halves_of(SLC[:]), tile_ps(t)).then_inc(tile_free[t.mod(2)], 1)
                        if c % 3 == 2:
                            act.wait_ge(tile_free[t.mod(2)], count_of(t.div(2) + 1))
                            e = (0 if i is None else i) * 4 + c // 3
                            copy(Hh[:, bass.ds(e, 1), :], Hf[:, bass.ds(e, 1), :]).then_inc(hh_ready, 1)
                    run(act, s, step)
                if s.name == "gu":
                    def step(c, i, s=s):
                        ahead(s, c, i)
                        t, cv = At(s.t0 + c, i, 4), At(s.cv0 + c // 2, i, 2)
                        if c % 2 == 0:
                            act.wait_ge(main_used, count_of(At(s.m0 + c + 1, i, 4)))
                            act.wait_ge(cv_seq, count_of(At(3 * (cv.base - 1), i, 6)))
                            act.wait_ge(tail_ready, count_of(cv + (-1)))
                            g = GP[:, c // 2, :]
                            for q, (dst, src) in enumerate(zip(padded(g), pieces(t))):
                                ins = copy(dst, src)
                            ins.then_inc(tile_free[t.mod(2)], 1)
                        else:
                            act.wait_ge(cv_seq, count_of(At(3 * (cv.base + 1), i, 6)))
                            act.activation(SLC[:, 0:NP_TOK], CV[:, 0:NP_TOK], ACT.Silu)
                            act.activation(seqs(SLC[:, NP_TOK:T]), convolved(CV)[2], ACT.Silu).then_inc(silu_ready, 1)
                            act.wait_ge(tile_free[t.mod(2)], count_of(t.div(2) + 1))
                            f = (0 if i is None else i) * 2 + c // 2
                            copy(Hh[:, bass.ds(f, 1), :], Hf[:, bass.ds(f, 1), :]).then_inc(hh_ready, 1)
                    run(act, s, step)
                if s.name == "qkv":
                    act.wait_ge(rows_out, 16 * count["rows"])
                    for c in range(s.n * s.body):
                        ahead(s, c, None)
                        t = At(s.t0 + c)
                        act.wait_ge(main_used, s.m0 + c + 1)
                        dst = (QF, KF, VF)[c // KT][:, c % KT, :]
                        act.activation(halves_of(dst), tile_ps(t), ACT.Copy, scale=0.125 if c < KT else 1.0)\
                           .then_inc(tile_free[t.mod(2)], 1)
                    attention(s)
                if s.name == "rwkv":
                    rwkv(s)
                if s.name == "g2":
                    gate(s)
                if s.name in ("out", "down"):
                    act.wait_ge(tail_ready, s.cv0)
                    for c in range(s.n * s.body):
                        ahead(s, c, None)
                        if c % s.per_tile == s.per_tile - 1:
                            e = c // s.per_tile
                            t = At(s.t0 + e)
                            act.wait_ge(main_used, s.m0 + c + 1)
                            square(tile_ps(t))
                            copy(halves_of(O[:, e, :]), tile_ps(t)).then_inc(tile_free[t.mod(2)], 1)
                    root()
                    bank = ps[0:HIST * NSEQ, TR, :]
                    if s.name == "out":
                        if s.layer % 3 == 0:
                            for g in range(2):
                                turned(rout[:, 512 * g:512 * (g + 1)], bank)
                            count["rows"] += 2
                        turned(ST[:], ps[:, TR, 0:FT * (3 + NB * HIST)].rearrange("p (g c) -> p g c", g=FT))
                    else:
                        for g in range(0, FT, 4):
                            w = min(4, FT - g) * P
                            turned(rout[:, g * P:g * P + w], bank[:, 0:w])
                        count["rows"] += 2
                    if s.m1 < SLOTS:
                        nxt = plan[plan.index(s) + 1]
                        pre_norm(nxt.name != "rwkv", nxt.halves)
                    else:
                        act.wait_ge(rows_out, 16 * count["rows"])
                        for g in range(5):
                            r = P if g < 4 else NS_TOK
                            for hh in range(2):
                                turned(yrow[0:r, g, 512 * hh:512 * (hh + 1)], ps[0:r, TR, :])

        @block.vector
        def _(dve):
            count = dict(seq=0, ss=0, u=0, half=0, tiles=0, x=0)

            def link(ins):
                ins.then_inc(dve_seq, 1)
                count["seq"] += 1
                dve.wait_ge(dve_seq, count["seq"])

            def split_lo(m, n):
                dve.wait_ge(hi_done, count_of(m + 1))
                dve.tensor_tensor(SL[:, m.mod(2)], raw[:, n.mod(4)], SH[:, m.mod(2)].bitcast(F32), ALU.subtract)\
                   .then_inc(lo_done, 1)

            def ahead(s, c, i):
                if i is None and s.m0 + c + 2 >= SLOTS:
                    return
                split_lo(At(s.m0 + c + 2, i, s.body), At(s.n0 + 24 * len(s.halves) + c + 2, i, s.body))

            def rms():
                count["ss"] += 1
                dve.wait_ge(sq_used, KT * count["ss"])
                dve.tensor_scalar(halves_of(RS[:]), ps[:, SS:SS + 2, 0:TH], 1.0 / D, EPS, ALU.mult, ALU.add)\
                   .then_inc(ss_read, 1)
                dve.wait_ge(root_done, count["ss"])
                link(dve.reciprocal(RS[:], RS[:]))

            def by_seq(half, m, k):
                return MOD[:, half % 3, m, k, 1:NSEQ].rearrange("p (s o) -> p s o", o=1).broadcast_to([P, NB, NT])

            def one(half, m, k):
                return MOD[:, half % 3, m, k, 0:1]

            def post_norm(half):
                rms()
                for k in range(KT):
                    if due(count["x"]):
                        dve.wait_ge(x_ready, count["x"])
                    link(dve.tensor_tensor(T1[:], O[:, k, :], RS[:], ALU.mult))
                    dve.scalar_tensor_tensor(X[:, k, 0:NP_TOK], T1[:, 0:NP_TOK], one(half, 2, k), X[:, k, 0:NP_TOK],
                                             ALU.mult, ALU.add)
                    ts = seqs(T1[:, NP_TOK:T])
                    link(dve.tensor_tensor(ts, ts, by_seq(half, 2, k), ALU.mult))
                    dve.tensor_tensor(X[:, k, NP_TOK:T], X[:, k, NP_TOK:T], T1[:, NP_TOK:T], ALU.add)\
                       .then_inc(x_ready, 1)
                    count["x"] += 1

            def pre_norm(half, split=True):
                rms()
                done, n0 = (uf_ready, count["u"]) if split else (ur_ready, 0)

                def low(k):
                    dve.wait_ge(uh_ready, count["u"] + k + 1)
                    dve.tensor_tensor(Ul[:, k, :], Uf[:, k, :], Uh[:, k, :].bitcast(F32), ALU.subtract)\
                       .then_inc(u_ready, 1)
                if due(count["x"]):
                    dve.wait_ge(x_ready, count["x"])
                for k in range(KT):
                    if k:
                        dve.wait_ge(done, n0 + k)
                    link(dve.tensor_tensor(T1[:], X[:, k, :], RS[:], ALU.mult))
                    ts = seqs(T1[:, NP_TOK:T])
                    link(dve.tensor_tensor(ts, ts, by_seq(half, 1, k), ALU.mult))
                    dve.tensor_scalar(Uf[:, k, 0:NP_TOK], T1[:, 0:NP_TOK], one(half, 1, k), one(half, 0, k),
                                      ALU.mult, ALU.add)
                    dve.tensor_tensor(seqs(Uf[:, k, NP_TOK:T]), ts, by_seq(half, 0, k), ALU.add).then_inc(done, 1)
                    if k and split:
                        low(k - 1)
                if not split:
                    return
                low(KT - 1)
                count["u"] += KT

            def take_mods():
                half = count["half"]
                count["half"] += 1
                l, h = half // 2, half % 2
                dve.wait_ge(ada_turned, half + 1)
                wide = lambda c: PT[:, :, c:c + 1].broadcast_to([P, KT, NSEQ])
                for m in range(3):
                    ins = dve.tensor_tensor(MOD[:, half % 3, m], ps[:, ADA, m * KT * NSEQ:(m + 1) * KT * NSEQ]
                                            .rearrange("p (k c) -> p k c", k=KT), wide(R_ADAB + 6 * l + 3 * h + m), ALU.add)
                link(ins)
                link(dve.scalar_tensor_tensor(MOD[:, half % 3, 1], MOD[:, half % 3, 1], 1.0,
                                              wide(R_NORM + 4 * l + 2 * h), ALU.add, ALU.mult))
                dve.tensor_tensor(MOD[:, half % 3, 2], MOD[:, half % 3, 2], wide(R_NORM + 4 * l + 2 * h + 1),
                                  ALU.mult).then_inc(mod_ready, 1)

            dve.wait_ge(tr_free, 2)
            dve.wait_ge(tr_free, 2 + KT + 1)
            take_mods()
            dve.wait_ge(mod_ready, 1)
            pre_norm(0)
            take_mods()
            for c in range(2):
                split_lo(*plan[0].slot(c, None))

            def convolve(g, cv0, step_i, w):
                for tap in range(3):
                    src = g[:, tap:tap + CW]
                    if tap == 0:
                        ins = dve.tensor_scalar(CV[:, 0:CW], src, w(0), None, ALU.mult)
                    else:
                        ins = dve.scalar_tensor_tensor(CV[:, 0:CW], src, w(tap), CV[:, 0:CW], ALU.mult, ALU.add)
                    ins.then_inc(cv_seq, 1)
                    if tap < 2:
                        dve.wait_ge(cv_seq, count_of(At(cv0 * 3 + tap + 1, *step_i)))

            def low_of_mix(s, e, mix):
                dve.wait_ge(hh_ready, count_of(mix + 1))
                at = bass.ds(e, 1)
                dve.tensor_tensor(Hl[:, at, :], Hf[:, at, :], Hh[:, at, :].bitcast(F32), ALU.subtract)\
                   .then_inc(mix_ready, 1)

            def attention(s):
                dve.wait_ge(misc_in, 32)
                dve.wait_ge(kv_out, 64)

                def biased(pc):
                    h, kb = pc // 4, 3 - pc % 4
                    w = NP_TOK - kb * P
                    z, e = ZB[:, pc % 2, 0:w], EX[:, pc % 2, 0:w]
                    dve.wait_ge(z_ready, pc + 1)
                    dve.tensor_scalar(z, ps[:, pc % 4, 0:w], BB[:, h:h + 1], None, ALU.add).then_inc(zb_ready, 1)
                    dve.wait_ge(zb_ready, pc + 1)
                    dve.scalar_tensor_tensor(e, z, -1.0, z, ALU.mult, ALU.max).then_inc(abs_ready, 1)

                def softplus(pc):
                    w = NP_TOK - (3 - pc % 4) * P
                    dve.wait_ge(ln_ready, pc + 1)
                    if due(pc - 1):
                        dve.wait_ge(cum_done, pc - 1)
                    if due(pc - 1):
                        dve.wait_ge(sum_ready, pc - 1)
                    dve.scalar_tensor_tensor(SP[:, pc % 2, 0:w], ZB[:, pc % 2, 0:w], 0.0, EX[:, pc % 2, 0:w],
                                             ALU.max, ALU.add).then_inc(sp_ready, 1)

                def take(p):
                    dve.wait_ge(av_done, 2 * p + 2)
                    dve.tensor_copy(Hf[:, p, 0:NP_TOK], ps[:, 4 + p % 2, :]).then_inc(av_read, 1)

                for k in range(4 * NH + 10):
                    if k < 4 * NH:
                        if due(k - 1):
                            dve.wait_ge(sp_ready, k - 1)
                        biased(k)
                    if 1 <= k < 4 * NH + 1:
                        softplus(k - 1)
                    if k % 8 == 5 and k >= 13:
                        take(k // 8 - 1)
                dve.wait_ge(cum_done, 4 * NH)
                dve.memset(QB[:], 0.0).then_inc(av_read, 1)
                dve.wait_ge(av_read, KT + 1)
                dve.tensor_copy(QB[0:HD, :, 0, :], QF[0:HD, :, NP_TOK:T])
                dve.tensor_copy(QB[HD:P, :, 1, :], QF[HD:P, :, NP_TOK:T]).then_inc(av_read, 1)

                def with_bias(out, bank, rows):
                    for a in range(2):
                        ins = dve.tensor_tensor(out[:, 512 * a:512 * a + 512].rearrange("p (k c) -> p k c", k=KT),
                                                ps[0:rows, bank + a, :].rearrange("p (k c) -> p k c", k=KT),
                                                BB[0:rows, KT * a:KT * a + KT].rearrange("p (k o) -> p k o", o=1)
                                                .broadcast_to([rows, KT, 64]), ALU.add)
                    return ins

                dve.wait_ge(kt_used, NB)
                for n, q in enumerate((2, 1, 0)):
                    rows = NS_TOK if q == 2 else P
                    bank = (4, 2, 0)[n]
                    z, e = SZ[0:rows, q, :], SE[0:rows, q, :]
                    with_bias(z, bank, rows).then_inc(szb, 1)
                    dve.wait_ge(szb, n + 1)
                    dve.scalar_tensor_tensor(e, z, -1.0, z, ALU.mult, ALU.max).then_inc(sabs, 1)
                for n, q in enumerate((2, 1, 0)):
                    rows = NS_TOK if q == 2 else P
                    z, e = SZ[0:rows, q, :], SE[0:rows, q, :]
                    dve.wait_ge(sln, n + 1)
                    dve.scalar_tensor_tensor(z, z, 0.0, e, ALU.max, ALU.add).then_inc(ssp, 1)
                for n, q in enumerate((2, 1, 0)):
                    rows = NS_TOK if q == 2 else P
                    bank = (4, 2, 0)[n]
                    dve.wait_ge(scum, n + 1)
                    with_bias(SE[0:rows, q, :], bank, rows).then_inc(sw, 1)
                dve.wait_ge(pages_used, NPAGE * NB)
                dve.tensor_copy(Hf[:, 0:KT, NP_TOK:T], ps[:, 6, :].rearrange("p (k c) -> p k c", k=KT))\
                   .then_inc(sav_read, 1)
                for e in range(KT):
                    dve.wait_ge(hh_ready, s.mix0 + e + 1)
                    dve.tensor_tensor(Hl[:, e, :], Hf[:, e, :], Hh[:, e, :].bitcast(F32), ALU.subtract)\
                       .then_inc(mix_ready, 1)

            def mix(mu, g):
                if due(KT * g):
                    dve.wait_ge(xm_ready, KT * g)
                for k in range(KT + 1):
                    if k < KT:
                        dve.scalar_tensor_tensor(XMf[:, k, :], Df[:, k, :], PT[:, k, R_MU + mu:R_MU + mu + 1],
                                                 Uf[:, k, :], ALU.mult, ALU.add).then_inc(xf_ready, 1)
                    if k:
                        dve.wait_ge(xh_ready, KT * g + k)
                        dve.tensor_tensor(XMl[:, k - 1, :], XMf[:, k - 1, :], XMh[:, k - 1, :].bitcast(F32),
                                          ALU.subtract).then_inc(xm_ready, 1)

            def project(s):
                dve.wait_ge(ur_ready, KT)
                for k in range(KT):
                    u, d = Uf[:, k, :], Df[:, k, :]
                    us, ds = seqs(u[:, NP_TOK:T]), seqs(d[:, NP_TOK:T])
                    dve.tensor_tensor(d[:, 1:NP_TOK], u[:, 0:NP_TOK - 1], u[:, 1:NP_TOK], ALU.subtract)
                    dve.tensor_scalar(d[:, 0:1], u[:, 0:1], -1.0, None, ALU.mult)
                    dve.tensor_tensor(ds[:, :, 1:NT], us[:, :, 0:NT - 1], us[:, :, 1:NT], ALU.subtract)
                    dve.tensor_tensor(ds[:, :, 0:1], PT[:, k, R_SSH:R_SSH + NB].rearrange("p (s o) -> p s o", o=1),
                                      us[:, :, 0:1], ALU.subtract).then_inc(xd_ready, 1)
                dve.wait_ge(xd_ready, KT)
                g = hd = 0
                for path, c, j, mu, t in lanes():
                    if mu is not None:
                        dve.wait_ge(main_used, s.m0 + c)
                        mix(mu, g)
                        g += 1
                    ahead(s, c, None)
                    if path in (W1, A1, G1):
                        hd += 1
                        dve.wait_ge(hd_ready, hd)
                        rows = 64 if path != G1 else 32 if j else P
                        f, h, l = (HDf, HDh, HDl) if path != G1 else (GHf[:, j], GHh[:, j], GHl[:, j])
                        dve.tensor_tensor(l[0:rows], f[0:rows], h[0:rows].bitcast(F32), ALU.subtract)\
                           .then_inc(hd_split, 1)

            def prepare(e):
                dve.tensor_tensor_scan(A_[:, e, :], RM[:], A_[:, e, :], 0.0, ALU.mult, ALU.add).then_inc(scanned, 1)
                dve.wait_ge(bs_out, e + 1)
                dve.tensor_scalar(halves_of(DR[:, e % 2, :]), ps[:, SS:SS + 2, 0:TH], 1e-24, None, ALU.max)\
                   .then_inc(bs_read, 1)

            def derive(e):
                par1 = lambda r: PT[:, e, r:r + 1]
                A, B, K, R = A_[:, e, :], B_[:, e, :], K_[:, e, :], R_[:, e, :]
                kk, by, ib, pb = DK[:, e % 2, :], DR[:, e % 2, :], IB[:, e % 2, :], PB[:, e % 2, :]
                dve.wait_ge(bs_rooted, e + 1)
                link(dve.reciprocal(by, by))
                link(dve.scalar_tensor_tensor(kk, K, par1(R_KK), by, ALU.mult, ALU.mult))
                link(dve.tensor_scalar(by, B, par1(R_KA), MKA[:, e:e + 1], ALU.mult, ALU.add))
                dve.tensor_tensor(K, K, by, ALU.mult)
                link(dve.tensor_tensor(B, B, kk, ALU.mult))
                dve.wait_ge(grown, e + 1)
                dve.tensor_copy(PC[:, e, 0:8], pb[:, HD - 1:NP_TOK:HD])
                dve.tensor_copy(PC[:, e, 8:16], pb[:, NP_TOK + NT - 1:T:NT])
                dve.tensor_tensor(K, K, ib, ALU.mult)
                dve.tensor_tensor(B, B, ib, ALU.mult)
                dve.tensor_tensor(R, R, pb, ALU.mult)
                link(dve.scalar_tensor_tensor(A[:, 1:T], kk[:, 1:T], -1.0, pb[:, 0:T - 1], ALU.mult, ALU.mult))
                dve.tensor_scalar(A[:, 0:NP_TOK:HD], kk[:, 0:NP_TOK:HD], -1.0, None, ALU.mult)
                link(dve.tensor_scalar(A[:, NP_TOK:T:NT], kk[:, NP_TOK:T:NT], -1.0, None, ALU.mult))

            def unit(w, q, i, pair, b):
                n, L, B = w.n, w.levels, w.bank
                dve.wait_ge(q.prod, count_of(At(1, i, 1)))
                mask = M2[0:n, int(not w.prompt), :, 0:n].rearrange("p (o x) t -> p o x t", o=1).broadcast_to([n, 2, 2, n])
                for h in range(2):
                    ins = dve.tensor_tensor(w.MM[:, h], ps[0:n, B + h, 0:4 * n].rearrange("p (k x t) -> p k x t", k=2, x=2),
                                            mask, ALU.mult)
                ins.then_inc(q.mm, 1)
                yield
                eye = ident[0:n, 0:n].rearrange("p (o t) -> p o t", o=1).broadcast_to([n, 2, n])
                dve.wait_ge(q.lva, count_of(At(1, i, L)))
                dve.tensor_tensor(w.TB[:, 0], ps[0:n, B, 0:2 * n].rearrange("p (h t) -> p h t", h=2), eye, ALU.add)
                dve.tensor_tensor(w.TB[:, 1], w.ML[:, 0], eye, ALU.add).then_inc(q.inv, 1)
                yield
                if not w.prompt:
                    seq = SAME[0:n, 3, 0:n:NT].rearrange("p (s o) -> p s o", o=1).broadcast_to([n, NB, HD])
                    wide = lambda a: a.rearrange("p (o k) -> p o k", o=1).broadcast_to([n, NB, HD])
                    dve.wait_ge(q.copied, count_of(At(1, i, L + 2)))
                    for h in range(2):
                        dve.tensor_tensor(w.BM[:, h], wide(w.TM[:, 1, HD * h:HD * h + HD]), seq, ALU.mult)
                        dve.tensor_tensor(w.VM[:, h], wide(w.TM[:, 3, HD * h:HD * h + HD]), seq, ALU.mult)
                flat = w.TB[:].rearrange("p x h t -> p (x h t)")
                for l in range(1, L):
                    part = slice(0 if l < L - 1 else 2 * n, 4 * n)
                    dve.wait_ge(q.inv, count_of(At(l, i, L)))
                    dve.wait_ge(q.lvt, count_of(At(l, i, L - 1)))
                    dve.tensor_tensor(flat[:, part], ps[0:n, B + 1, part], flat[:, part], ALU.add).then_inc(q.inv, 1)
                    yield
                if not w.prompt:
                    dve.wait_ge(q.copied, count_of(At(L + 2, i, L + 2)))
                    for h in range(2):
                        ins = dve.tensor_tensor(w.UM[:, h], wide(w.UW[:, h, 0, :]), seq, ALU.mult)
                    ins.then_inc(q.umask, 1)
                dve.wait_ge(q.rgh, count_of(At(1, i, 1)))
                dve.tensor_tensor(w.RP[:], w.FS[:, 1], ps[:, B + 2, 0:n], ALU.add)
                if w.prompt:
                    for c in range(2):
                        ins = dve.tensor_tensor(w.GG[:, c], ps[:, B + (3, 1)[c], 0:HD], J2[:], ALU.add)
                    ins.then_inc(q.rp, 1)
                    yield
                    for c in range(2):
                        dve.wait_ge(q.chain, count_of(At(c + 1, i, 2)))
                        dve.tensor_scalar(w.SC[:], ps[:, B + (3, 1)[c], HD:P], chunk_end(pair, b, c), None, ALU.mult)\
                           .then_inc(q.state, 1)
                        yield
                    dve.wait_ge(q.state, count_of(At(2, i, 2)))
                    dve.tensor_copy(SF[:, bass.ds(pair, 1), :].rearrange("p a v -> p (a v)"), w.SC[:]).then_inc(q.free, 1)
                else:
                    j2 = J2[:].rearrange("p (o k) -> p o k", o=1).broadcast_to([P, NB, HD])
                    by_s = lambda a: a.rearrange("p (s k) -> p s k", s=NB)
                    dve.tensor_tensor(w.GG[:], by_s(ps[:, 6, :]), j2, ALU.add).then_inc(q.rp, 1)
                    dve.wait_ge(q.chain, count_of(At(1, i, 1)))
                    ends = PC[:, bass.ds(pair, 1), 8:16].rearrange("p a (s o) -> p (a s) o", o=1).broadcast_to([P, NB, HD])
                    dve.tensor_tensor(w.S1[:], by_s(ps[:, 4, :]), ends, ALU.mult).then_inc(q.state, 1)
                    dve.wait_ge(q.state, count_of(At(1, i, 1)))
                    dve.sem_inc(q.free, 1)
                yield

            def no_state(g, pp):
                dve.wait_ge(QP[g].free, count_of(At(1, pp, NP_TOK // P)))
                dve.tensor_copy(WP[g].SC[:], ZERO[:])

            def rwkv(s):
                project(s)
                dve.wait_ge(tile_free[0], s.t1 // 2)
                dve.wait_ge(tile_free[1], s.t1 // 2)
                dve.wait_ge(mask_ready, 1)
                link(dve.tensor_scalar(MKA[:], PT[:, :, R_KA], -1.0, 1.0, ALU.mult, ALU.add))
                prepare(0)
                for e in range(KT):
                    if e < KT - 1:
                        prepare(e + 1)
                    derive(e)
                for w, q in zip(WP, QP):
                    dve.tensor_copy(w.SC[:], ZERO[:]).then_inc(q.free, 1)
                prompt_units(dve, unit, no_state)
                dve.wait_ge(so_ready, 1)
                dve.tensor_copy(WS.S1[:, 0, :], ZERO[:]).then_inc(QS.free, 1)
                sample_units(dve, unit)

            def gate(s):
                n = [KT]

                def sums(f, done=bs_read):
                    n[0] += 1
                    dve.wait_ge(bs_out, n[0])
                    return f(ps[:, SS:SS + 2, 0:TH]).then_inc(done, 1)

                dve.wait_ge(QS.y, KT + 1)
                dve.wait_ge(wkv_out, 16 + 32 * KT)
                for e in range(KT):
                    par1 = lambda r: PT[:, e, r:r + 1]
                    sums(lambda a: dve.scalar_tensor_tensor(halves_of(T1[:]), a, -1.0 / HD, halves_of(A_[:, e, :]),
                                                            ALU.mult, ALU.add))
                    dve.scalar_tensor_tensor(SQ[:, 1, :], R_[:, e, :], par1(R_RK), K_[:, e, :], ALU.mult, ALU.mult)\
                       .then_inc(bs_in2, 1)
                    sums(lambda a: dve.tensor_scalar(halves_of(RS[:]), a, 1.0 / HD, GN_EPS, ALU.mult, ALU.add))
                    dve.wait_ge(bs_rooted, KT + e + 1)
                    link(dve.reciprocal(RS[:], RS[:]))
                    link(dve.tensor_tensor(T1[:], T1[:], RS[:], ALU.mult))
                    link(dve.tensor_scalar(T1[:], T1[:], par1(R_LNW), par1(R_LNB), ALU.mult, ALU.add))
                    sums(lambda a: dve.tensor_tensor(halves_of(SQ[:, 1, :]), a, halves_of(V_[:, e, :]), ALU.mult))
                    dve.wait_ge(bs_read, n[0])
                    link(dve.tensor_tensor(T1[:], T1[:], SQ[:, 1, :], ALU.add))
                    t = At(s.t0 + e)
                    if e < KT - 1:
                        dve.wait_ge(lr_tile, 2 * (KT - 1) + e + 1)
                    else:
                        dve.wait_ge(main_used, s.m1)
                    dve.tensor_tensor(halves_of(XMf[:, e, :]), halves_of(T1[:]), tile_ps(t), ALU.mult)\
                       .then_inc(tile_free[t.mod(2)], 1)
                    dve.wait_ge(hh_ready, s.mix0 + e + 1)
                    dve.tensor_tensor(XMl[:, e, :], XMf[:, e, :], XMh[:, e, :].bitcast(F32), ALU.subtract)\
                       .then_inc(mix_ready, 1)
                for c in range(2):
                    ahead(s, c, None)

            for s in plan:
                if s.name == "rwkv":
                    rwkv(s)
                if s.name == "g2":
                    gate(s)
                if s.name == "qkv":
                    run(dve, s, lambda c, i, s=s: ahead(s, c, i))
                    attention(s)
                if s.name in ("in", "gu"):
                    dve.wait_ge(sq_used, KT * count["ss"])
                if s.name == "in":
                    j = s.layer // 3

                    def step(c, i, s=s):
                        ahead(s, c, i)
                        t, cv = At(s.t0 + c, i, 12), At(s.cv0 + c // 3, i, 4)
                        e = (0 if i is None else i) * 4 + c // 3
                        g = GP[:, c // 3 % 2, :]
                        if c % 3 == 1:
                            dve.wait_ge(main_used, count_of(At(s.m0 + c + 1, i, 12)))
                            before = t + (-1)
                            dve.wait_ge(tile_free[before.mod(2)], count_of(before.div(2) + 1))
                            if due(cv + (-1)):
                                dve.wait_ge(tail_ready, count_of(cv + (-1)))
                            gate = (SLC[:, 0:TH], SLC[:, TH:NP_TOK], seqs(SLC[:, NP_TOK:T]))
                            for dst, src, by in zip(padded(g), pieces(t), gate):
                                ins = dve.tensor_tensor(dst, src, by, ALU.mult)
                            ins.then_inc(tile_free[t.mod(2)], 1)
                            dve.wait_ge(tile_free[t.mod(2)], count_of(t.div(2) + 1))
                            dve.wait_ge(pad_ready, count_of(cv + 1))
                            w = lambda tap: PT[:, bass.ds(e, 1), R_CONVA + 3 * j + tap:R_CONVA + 3 * j + tap + 1]\
                                .rearrange("p a b -> p (a b)")
                            convolve(g, cv.base, (i, 12), w)
                        if c % 3 == 2:
                            dve.wait_ge(main_used, count_of(At(s.m0 + c + 1, i, 12)))
                            dve.wait_ge(cv_seq, count_of(At(3 * (cv.base + 1), i, 12)))
                            dst = Hf[:, bass.ds(e, 1), :].rearrange("p a t -> p (a t)")
                            dsts = (dst[:, 0:TH], dst[:, TH:NP_TOK], seqs(dst[:, NP_TOK:T]))
                            for d, src, by in zip(dsts, pieces(t), convolved(CV)):
                                ins = dve.tensor_tensor(d, src, by, ALU.mult)
                            ins.then_inc(tile_free[t.mod(2)], 1)
                            low_of_mix(s, e, At(s.mix0 + c // 3, i, 4))
                    run(dve, s, step)
                if s.name == "gu":
                    def step(c, i, s=s):
                        ahead(s, c, i)
                        t, cv = At(s.t0 + c, i, 4), At(s.cv0 + c // 2, i, 2)
                        f = (0 if i is None else i) * 2 + c // 2
                        if c % 2 == 0:
                            dve.wait_ge(tile_free[t.mod(2)], count_of(t.div(2) + 1))
                            dve.wait_ge(pad_ready, count_of(cv + 1))
                            dve.wait_ge(silu_ready, count_of(At(1 + FT * s.layer + c // 2, i, 2)))
                            w = lambda tap: ST[:, bass.ds(f, 1), tap:tap + 1].rearrange("p a b -> p (a b)")
                            convolve(GP[:, c // 2, :], cv.base, (i, 6), w)
                        else:
                            dve.wait_ge(main_used, count_of(At(s.m0 + c + 1, i, 4)))
                            dve.wait_ge(silu_ready, count_of(At(2 + FT * s.layer + c // 2, i, 2)))
                            dst = Hf[:, bass.ds(f, 1), :].rearrange("p a (h t) -> p (a h) t", h=2)
                            dve.tensor_tensor(dst, tile_ps(t), halves_of(SLC[:]), ALU.mult)\
                               .then_inc(tile_free[t.mod(2)], 1)
                            low_of_mix(s, f, At(s.mix0 + c // 2, i, 2))
                    run(dve, s, step)
                if s.name in ("out", "down"):
                    for c in range(s.n * s.body):
                        ahead(s, c, None)
                    dve.wait_ge(mod_ready, count["half"])
                    if s.name == "out":
                        if s.layer % 3 == 2:
                            dve.wait_ge(x_back, 16)
                        dve.wait_ge(tile_free[0], s.t1 // 2)
                        dve.wait_ge(tile_free[1], s.t1 // 2)
                        post_norm(2 * s.layer)
                        pre_norm(2 * s.layer + 1)
                    else:
                        dve.wait_ge(tile_free[0], s.t1 // 2)
                        dve.wait_ge(tile_free[1], s.t1 // 2)
                        post_norm(2 * s.layer + 1)
                        if s.m1 < SLOTS:
                            pre_norm(2 * s.layer + 2, plan[plan.index(s) + 1].name != "rwkv")
                    if s.m1 < SLOTS and plan[plan.index(s) + 1].halves:
                        take_mods()

        @block.gpsimd
        def _(pool):
            count = dict(rows_out=0, tr=11, seq=1)
            pool.memset(ones[:], 1.0)
            pool.memset(nones[:], -1.0)
            pool.memset(ntri[:], -1.0)
            pool.memset(ident[:], 0.0).then_inc(pool_seq, 1)
            pool.wait_ge(pool_seq, 1)
            pool.affine_select(out=ntri[:], in_=ntri[:], compare_op=ALU.is_ge, fill=0.0, base=0,
                               pattern=[[-1, P]], channel_multiplier=1)
            pool.affine_select(out=ident[:], in_=ident[:], compare_op=ALU.not_equal, fill=1.0, base=0,
                               pattern=[[-1, P]], channel_multiplier=1).then_inc(const_ready, 1)
            for dst, src in par_rows(x):
                pool.dma_start(par[dst:dst + src.shape[0], :], src).then_inc(par_in, 16)
            pool.dma_start(pages[:], x["page_table"].rearrange("(o b) j -> o (b j)", o=1)).then_inc(misc_in, 16)
            pool.dma_start(BB[:], x["b_bias"].broadcast_to([P, NH])).then_inc(misc_in, 16)
            pool.dma_start(xrow[:, 0:4, :], x["x_prompt"][0].rearrange("(g p) d -> p g d", p=P)).then_inc(x_in, 16)
            pool.dma_start(xrow[0:NS_TOK, 4, :], x["x_sample"].rearrange("b t d -> (b t) d")).then_inc(x_in, 16)

            def rows(r, n, base, prompt, sample):
                pool.wait_ge(tr_free, count["tr"])
                pool.dma_start(prompt, rout[0:HIST, 0:n]).then_inc(rows_out, 16)
                pool.dma_start(sample, rout[HIST:HIST * NSEQ, 0:n]).then_inc(rows_out, 16)
                count["rows_out"] += 2

            def keep(s, idx, g, f, pads, free, i):
                if due(At(3 * (idx.base - 1), i, 3 * idx.step)):
                    pool.wait_ge(cv_seq, count_of(At(3 * (idx.base - 1), i, 3 * idx.step)))
                pool.tensor_copy(seqs(GP[:, g, SROW:PADW])[:, :, 0:HIST], pads).then_inc(pad_ready, 1)
                free()
                tl = TL[:, bass.ds(f, 1), :].rearrange("p a c -> p (a c)")
                pool.tensor_copy(tl[:, 0:HIST], GP[:, g, NP_TOK:NP_TOK + HIST])
                pool.tensor_copy(tl[:, HIST:].rearrange("p (s r) -> p s r", s=NB),
                                 seqs(GP[:, g, SROW:PADW])[:, :, NT:NT + HIST]).then_inc(tail_ready, 1)

            def attention(s):
                t0 = count["tr"]
                flat = lambda a: a.rearrange("b t h d -> (b t) (h d)")
                blocks = lambda a: flat(a).rearrange("(g p) d -> p g d", p=P)
                pool.wait_ge(tr_free, t0 + 10)
                pool.dma_start(blocks(o["v_prompt"][0]), VT[:, 0:4, :]).then_inc(kv_out, 16)
                pool.dma_start(flat(o["v_sample"][0]), VT[0:NS_TOK, 4, :]).then_inc(kv_out, 16)
                pool.wait_ge(tr_free, t0 + 20)
                pool.dma_start(blocks(o["k_prompt"][0]), KR[:]).then_inc(kv_out, 16)
                pool.dma_start(flat(o["k_sample"][0]), KS[:]).then_inc(kv_out, 16)
                count["tr"] += 20
                pool.wait_ge(misc_in, 32)
                page = [pool.value_load(pages[0:1, n:n + 1], min_val=0, max_val=x["cache_k"].shape[1] - 1)
                        for n in range(NB * NPAGE)]

                def load_page(n):
                    cache = x["cache_k"] if n < NB * NPAGE else x["cache_v"]
                    if n < NB * NPAGE:
                        if due(2 * (n - 3)):
                            pool.wait_ge(kt_full, 2 * (n - 3))
                    elif n - 4 < NB * NPAGE:
                        pool.wait_ge(kt_full, 2 * (n - 3))
                    else:
                        pool.wait_ge(pages_used, n - 3 - NB * NPAGE)
                    pool.dma_start(PG[:, n % 4, :], cache[0, bass.ds(page[n % (NB * NPAGE)], 1)]
                                   .rearrange("o t h d -> (o t) (h d)")).then_inc(page_full[n % 4], 16)

                def mask_sp(pc):
                    h, kb = pc // 4, 3 - pc % 4
                    w = NP_TOK - kb * P
                    pool.wait_ge(sp_ready, pc + 1)
                    d = SP[:, pc % 2, 0:P]
                    pool.affine_select(out=d, in_=d, compare_op=ALU.is_gt, fill=0.0, base=0, pattern=[[1, P]],
                                       channel_multiplier=-1).then_inc(spm_ready, 1)
                    pool.wait_ge(spm_ready, pc + 1)
                    if due(pc):
                        pool.wait_ge(cum_done, pc)
                    ins = pool.tensor_copy(SUM[:, pc % 2, 0:P], d)
                    if kb < 3:
                        ins = pool.tensor_tensor(SUM[:, pc % 2, P:w], SUM[:, (pc - 1) % 2, 0:w - P],
                                                 SP[:, pc % 2, P:w], ALU.add)
                    ins.then_inc(sum_ready, 1)
                    pool.wait_ge(sum_ready, pc + 1)

                def mask_a(pc):
                    h, kb = pc // 4, 3 - pc % 4
                    o0 = (0, P, 3 * P, 6 * P)[3 - kb]
                    pool.wait_ge(a_ready, pc + 1)
                    d = AT[:, h % 2, o0:o0 + P]
                    pool.affine_select(out=d, in_=d, compare_op=ALU.is_gt, fill=0.0, base=0, pattern=[[1, P]],
                                       channel_multiplier=-1).then_inc(am_ready, 1)

                for k in range(4 * NH + 3):
                    if k < 4 * NH:
                        mask_sp(k)
                    if k >= 3:
                        mask_a(k - 3)

                def same_sequence(a):
                    v = a.rearrange("p (h s t) -> p h s t", h=NH, s=NB)
                    pool.affine_select(out=v, in_=v, compare_op=ALU.is_ge, fill=0.0, base=0,
                                       pattern=[[0, NH], [-NT, NB], [0, NT]], channel_multiplier=1).then_inc(pool_seq, 1)
                    count["seq"] += 1
                    pool.wait_ge(pool_seq, count["seq"])
                    return pool.affine_select(out=v, in_=v, compare_op=ALU.is_gt, fill=0.0, base=0,
                                              pattern=[[0, NH], [NT, NB], [1, NT]], channel_multiplier=-1)

                pool.wait_ge(av_done, NH)
                pool.wait_ge(kv_out, 64)
                for n in range(NB * NPAGE + 4):
                    load_page(n)
                pool.wait_ge(ssp, 1)
                same_sequence(SZ[0:NS_TOK, 2, :]).then_inc(sspm, 1)
                for q in (1, 0):
                    pool.wait_ge(ssp, 3 - q)
                    pool.engine_nop().then_inc(sspm, 1)
                pool.wait_ge(sa, 1)
                same_sequence(SE[0:NS_TOK, 2, :]).then_inc(sam, 1)
                for q in (1, 0):
                    pool.wait_ge(sa, 3 - q)
                    pool.engine_nop().then_inc(sam, 1)
                for n in range(NB * NPAGE + 4, 2 * NB * NPAGE):
                    load_page(n)

            def masks():
                def linked(ins):
                    ins.then_inc(pool_seq, 1)
                    count["seq"] += 1
                    pool.wait_ge(pool_seq, count["seq"])

                linked(pool.memset(SAME[:], 1.0))
                for l in range(7):
                    B = 2 ** l
                    v = SAME[:, l, :].rearrange("p (c t) -> p c t", t=B)
                    for base, sign in ((0, 1), (B - 1, -1)):
                        linked(pool.affine_select(out=v, in_=v, compare_op=ALU.is_ge, fill=0.0, base=base,
                                                  pattern=[[-B * sign, P // B], [0, B]], channel_multiplier=sign))
                pool.tensor_tensor(LM[:], SAME[:, 1:7, :], SAME[:, 0:6, :], ALU.subtract)
                for ph, l in ((0, 6), (1, 3)):
                    for q in range(2):
                        linked(pool.tensor_copy(M2[:, ph, q, :], SAME[:, l, :]))
                        linked(pool.affine_select(out=M2[:, ph, q, :], in_=M2[:, ph, q, :],
                                                  compare_op=(ALU.is_gt, ALU.is_ge)[q], fill=0.0, base=0,
                                                  pattern=[[1, P]], channel_multiplier=-1))
                pool.tensor_tensor(J2[:], ident[:, 0:HD], ident[:, HD:P], ALU.add)
                pool.memset(ZERO[:], 0.0)
                linked(pool.memset(RM[:], 1.0))
                pool.memset(RM[:, 0:NP_TOK:HD], 0.0)
                pool.memset(RM[:, NP_TOK:T:NT], 0.0).then_inc(mask_ready, 1)

            def unit(w, q, i, pair, b):
                n, L = w.n, w.levels
                if not w.prompt:
                    pool.wait_ge(q.free, count_of(At(1, i, 1)))
                    settle(pool)
                    for h in range(2):
                        pool.dma_start(w.SN[:, :, HD * h:HD * h + HD], x["state_wkv"][0][:, bass.ds(pair * 2 + h, 1)]
                                       .rearrange("b h i j -> i (b h) j")).then_inc(sn_in, 16)
                pool.wait_ge(q.mm, count_of(At(1, i, 1)))
                for l in range(L):
                    if l >= 2:
                        pool.wait_ge(q.lva, count_of(At(l - 1, i, L)))
                        if l == 2:
                            pool.wait_ge(q.inv, count_of(At(1, i, L)))
                    lm = LM[0:n, l, 0:n].rearrange("p (o t) -> p o t", o=1).broadcast_to([n, 2, n])
                    pool.tensor_tensor(w.ML[:, l % 2], w.MM[:, :, 0, 0, :], lm, ALU.mult).then_inc(q.ml, 1)
                    yield
                if not w.prompt:
                    pool.wait_ge(sn_back, count_of(At(1, i, 1)))
                    settle(pool)
                    for h in range(2):
                        pool.dma_start(o["wkv_sample"][0][:, bass.ds(pair * 2 + h, 1)].rearrange("b h i j -> i (b h) j"),
                                       w.SN[:, :, HD * h:HD * h + HD]).then_inc(wkv_out, 16)
                    pool.wait_ge(wkv_out, count_of(At(48, i, 32)))

            def rwkv(s):
                pool.wait_ge(x_ready, KT * 2 * s.layer)
                pool.dma_start(XS, X[:]).then_inc(spilled, 16)
                pool.wait_ge(tr_free, count["tr"] + 2)
                count["tr"] += 2
                pool.dma_start(o["shift_prompt"][0], SHR[0:1, :]).then_inc(shift_out, 16)
                pool.dma_start(o["shift_sample"][0], SHR[1:, :]).then_inc(shift_out, 16)
                pool.wait_ge(xm_ready, 6 * KT)
                masks()
                prompt_units(pool, unit)
                pool.wait_ge(so_ready, 1)
                pool.dma_start(o["wkv_prompt"][0, 0].rearrange("h i j -> i h j"),
                               SO[:].rearrange("p e (r j) -> p (e r) j", r=2)).then_inc(wkv_out, 16)
                pool.wait_ge(wkv_out, 16)
                sample_units(pool, unit)
                pool.wait_ge(bs_in2, KT)
                pool.dma_start(X[:], XS).then_inc(x_back, 16)

            for s in plan:
                if s.name == "rwkv":
                    rwkv(s)
                if s.name == "qkv":
                    attention(s)
                if s.name in ("in", "gu"):
                    pool.wait_ge(sq_used, KT + 4 * KT * s.layer + (2 * KT if s.name == "gu" else 0))
                    pool.wait_ge(tr_full, count["tr"])
                    pool.wait_ge(tr_free, count["tr"])
                    pool.memset(GP[:, :, 0:HIST], 0.0)
                if s.name == "in":
                    j = s.layer // 3

                    def step(q, i, s=s):
                        e = (0 if i is None else i) * 4 + q
                        t = At(s.t0 + 3 * q + 1, i, 12)
                        pads = PT[:, bass.ds(e, 1), R_STA + 16 * j:R_STA + 16 * j + 16]\
                            .rearrange("p a (s r) -> p (a s) r", s=NB)
                        keep(s, At(s.cv0 + q, i, 4), q % 2, e, pads,
                             lambda: pool.wait_ge(tile_free[t.mod(2)], count_of(t.div(2) + 1)), i)
                    run(pool, s, step, 4)
                if s.name == "gu":
                    def step(q, i, s=s):
                        f = (0 if i is None else i) * 2 + q
                        t = At(s.t0 + 2 * q, i, 4)
                        pads = ST[:, bass.ds(f, 1), 3:3 + NB * HIST].rearrange("p a (s r) -> p (a s) r", s=NB)
                        keep(s, At(s.cv0 + q, i, 2), q, f, pads,
                             lambda: pool.wait_ge(tile_free[t.mod(2)], count_of(t.div(2) + 1)), i)
                    run(pool, s, step, 2)
                if s.name == "out":
                    l = s.layer
                    pool.wait_ge(main_used, s.m1)
                    pool.dma_start(srow[0:3, :], x["f_conv"][l]).then_inc(rows_in, 16)
                    pool.dma_start(srow[3:, :], x["state_ffn_conv"][l].rearrange("b r f -> (b r) f")).then_inc(rows_in, 16)
                    if l % 3 == 0:
                        count["tr"] += 2
                        rows(0, D, 0, o["conv_a_prompt"][l // 3, 0], o["conv_a_sample"][l // 3].rearrange("b r d -> (b r) d"))
                    count["tr"] += 1
                if s.name == "down":
                    l = s.layer
                    count["tr"] += 6
                    rows(0, F, 0, o["ffn_conv_prompt"][l, 0], o["ffn_conv_sample"][l].rearrange("b r f -> (b r) f"))
            pool.wait_ge(tr_free, count["tr"] + 10)
            pool.dma_start(o["y_prompt"][0].rearrange("(g p) d -> p g d", p=P), yrow[:, 0:4, :]).then_inc(rows_out, 16)
            pool.dma_start(o["y_sample"].rearrange("b t d -> (b t) d"), yrow[0:NS_TOK, 4, :]).then_inc(rows_out, 16)
            pool.wait_ge(rows_out, 16 * (count["rows_out"] + 2))


_INS = ['x_prompt', 'x_sample', 'cache_k', 'cache_v', 'page_table', 'state_conv_a', 'state_wkv', 'state_shift',
        'state_ffn_conv', 'c_prompt', 'c_sample', 'ada_w', 'ada_b', 'norm_g', 'a_w_in', 'a_conv', 'a_w_out',
        'b_w_qkv', 'b_w_o', 'b_bias', 'r7_mu', 'r7_w_rkv', 'r7_w0', 'r7_w1', 'r7_w2', 'r7_a0', 'r7_a1', 'r7_a2',
        'r7_g1', 'r7_g2', 'r7_k_k', 'r7_k_a', 'r7_r_k', 'r7_ln_w', 'r7_ln_b', 'r7_w_o', 'f_w_gu', 'f_conv',
        'f_w_down']
_OUTS = [('y_prompt', (1, 512, 1024)), ('y_sample', (8, 8, 1024)),
         ('k_prompt', (1, 1, 512, 16, 64)), ('v_prompt', (1, 1, 512, 16, 64)),
         ('k_sample', (1, 8, 8, 16, 64)), ('v_sample', (1, 8, 8, 16, 64)),
         ('conv_a_prompt', (2, 1, 2, 1024)), ('conv_a_sample', (2, 8, 2, 1024)),
         ('wkv_prompt', (1, 1, 16, 64, 64)), ('wkv_sample', (1, 8, 16, 64, 64)),
         ('shift_prompt', (1, 1, 1024)), ('shift_sample', (1, 8, 1024)),
         ('ffn_conv_prompt', (4, 1, 2, 2816)), ('ffn_conv_sample', (4, 8, 2, 2816))]


def kernel(**inputs):
    import numpy as np
    import concourse.bacc as bacc
    from concourse.bass_utils import run_bass_kernel_spmd as run

    nc = bacc.Bacc("TRN2", target_bir_lowering=False, num_devices=1)
    arrays, ins, outs = {}, {}, {}
    for name in _INS:
        a = np.ascontiguousarray(inputs[name])
        arrays["in_" + name] = a
        ins[name] = nc.dram_tensor("in_" + name, a.shape, mybir.dt.from_np(a.dtype), kind="ExternalInput").ap()
    for name, shape in _OUTS:
        outs[name] = nc.dram_tensor("out_" + name, shape, F32, kind="ExternalOutput").ap()
    trunk_program(nc, ins, outs)
    r = run(nc, [arrays], core_ids=[0])
    return tuple(r.results[0]["out_" + name] for name, _ in _OUTS)
```
